# Optimizing a Trainium2 kernel written in Bass

```python
import jax, jax.numpy as jnp
from jax import lax
import numpy as np

D_MODEL = 2048
BATCH = 1
SEQ = 256
DEPTH = 2

GRID_W = 64
CTX_LEN = 256
N_MIXERS = 2
N_HEADS = 16
N_KV_HEADS = 4
HEAD_DIM = D_MODEL // N_HEADS
KV_GROUP = N_HEADS // N_KV_HEADS
KV_DIM = N_KV_HEADS * HEAD_DIM
QKV_DIM = D_MODEL + 2 * KV_DIM
ROPE_THETA = 10000.0
Q_BLOCK = 128
N_FOURIER_GROUPS = 8
FOURIER_GROUP_DIM = D_MODEL // N_FOURIER_GROUPS
D_FF = 4 * D_MODEL
N_MOD = 6
EPS = 1e-6
N_ATTN_LAYERS = (DEPTH + N_MIXERS - 1) // N_MIXERS
N_FOURIER_LAYERS = DEPTH // N_MIXERS

kernel_name = "hybrid_gqa_fourier_dit_block"

def rms_norm(x, g):
    xf = x.astype(jnp.float32)
    y = xf * lax.rsqrt(jnp.mean(xf * xf, axis=-1, keepdims=True) + EPS)
    return (y * g.astype(jnp.float32)).astype(x.dtype)

def modulate(h, shift, scale):
    return h * (1 + scale) + shift

def axial_rope_angles(n_tokens):
    rows = n_tokens // GRID_W
    row = jnp.broadcast_to(jnp.arange(rows)[:, None], (rows, GRID_W)).reshape(-1)
    col = jnp.broadcast_to(jnp.arange(GRID_W)[None, :], (rows, GRID_W)).reshape(-1)
    n_freq = HEAD_DIM // 4
    inv_freq = ROPE_THETA ** (-jnp.arange(n_freq, dtype=jnp.float32) / n_freq)
    ang = jnp.concatenate([row.astype(jnp.float32)[:, None] * inv_freq,
                           col.astype(jnp.float32)[:, None] * inv_freq], axis=-1)
    return jnp.cos(ang), jnp.sin(ang)

def apply_rope(x, cos, sin):
    xp = x.astype(jnp.float32).reshape(x.shape[:-1] + (HEAD_DIM // 2, 2))
    x0, x1 = xp[..., 0], xp[..., 1]
    c = cos[None, :, None, :]
    s = sin[None, :, None, :]
    out = jnp.stack([x0 * c - x1 * s, x0 * s + x1 * c], axis=-1)
    return out.reshape(x.shape).astype(x.dtype)

def project_kv(h, w_kv, k_gain):
    b, n, _ = h.shape
    kv = h @ w_kv
    k, v = jnp.split(kv, 2, axis=-1)
    k = rms_norm(k.reshape(b, n, N_KV_HEADS, HEAD_DIM), k_gain)
    v = v.reshape(b, n, N_KV_HEADS, HEAD_DIM)
    return k, v

def project_qkv(h, w_qkv, q_gain, k_gain):
    b, n, _ = h.shape
    q = rms_norm((h @ w_qkv[:, :D_MODEL]).reshape(b, n, N_HEADS, HEAD_DIM), q_gain)
    k, v = project_kv(h, w_qkv[:, D_MODEL:], k_gain)
    return q, k, v

def latent_attention(q_lat, k_lat, v_lat, k_ctx, v_ctx):
    b, s = q_lat.shape[:2]
    n_blocks = s // Q_BLOCK
    qb = jnp.moveaxis(q_lat.reshape(b, n_blocks, Q_BLOCK, N_KV_HEADS, KV_GROUP, HEAD_DIM), 1, 0)
    scale = HEAD_DIM ** -0.5

    def one_block(q):
        logits = jnp.concatenate([
            jnp.einsum('bqkgd,bskd->bkgqs', q, k_lat),
            jnp.einsum('bqkgd,bskd->bkgqs', q, k_ctx)], axis=-1).astype(jnp.float32) * scale
        p = jax.nn.softmax(logits, axis=-1).astype(v_lat.dtype)
        return (jnp.einsum('bkgqs,bskd->bqkgd', p[..., :s], v_lat)
                + jnp.einsum('bkgqs,bskd->bqkgd', p[..., s:], v_ctx))

    o = lax.map(one_block, qb)
    return jnp.moveaxis(o, 0, 1).reshape(b, s, D_MODEL)

def context_attention(q_ctx, k_ctx, v_ctx):
    b, l = q_ctx.shape[:2]
    q = q_ctx.reshape(b, l, N_KV_HEADS, KV_GROUP, HEAD_DIM)
    logits = jnp.einsum('bqkgd,bskd->bkgqs', q, k_ctx).astype(jnp.float32) * (HEAD_DIM ** -0.5)
    p = jax.nn.softmax(logits, axis=-1).astype(v_ctx.dtype)
    return jnp.einsum('bkgqs,bskd->bqkgd', p, v_ctx).reshape(b, l, D_MODEL)

def fourier_mix(h, w_o):
    b, n, _ = h.shape
    hg = h.astype(jnp.float32).reshape(b, n, N_FOURIER_GROUPS, FOURIER_GROUP_DIM)
    y = jnp.fft.fftn(hg, axes=(1, 3), norm="ortho").real
    return y.reshape(b, n, D_MODEL).astype(h.dtype) @ w_o

def sq_relu_mlp(h, w1, w2):
    return jnp.square(jax.nn.relu(h @ w1)) @ w2

def setup_inputs(seed: int = 0) -> dict:
    key = jax.random.key(seed)
    ks = jax.random.split(key, 16)
    f32 = jnp.float32

    def normal(k, shape, std):
        return jax.random.normal(k, shape, f32) * std

    return {
        "x": normal(ks[0], (BATCH, SEQ, D_MODEL), 1.0),
        "c": normal(ks[1], (BATCH, D_MODEL), 1.0),
        "ctx": normal(ks[2], (BATCH, CTX_LEN, D_MODEL), 1.0),
        "c_ctx": normal(ks[3], (D_MODEL,), 1.0),
        "ada_w": normal(ks[4], (DEPTH, D_MODEL, N_MOD * D_MODEL), 0.02),
        "ada_b": normal(ks[5], (DEPTH, N_MOD * D_MODEL), 0.05),
        "norm_mix_g": 1.0 + normal(ks[6], (DEPTH, D_MODEL), 0.02),
        "norm_mlp_g": 1.0 + normal(ks[7], (DEPTH, D_MODEL), 0.02),
        "attn_w_qkv": normal(ks[8], (N_ATTN_LAYERS, D_MODEL, QKV_DIM), D_MODEL ** -0.5),
        "attn_q_norm_g": 1.0 + normal(ks[9], (N_ATTN_LAYERS, HEAD_DIM), 0.02),
        "attn_k_norm_g": 1.0 + normal(ks[10], (N_ATTN_LAYERS, HEAD_DIM), 0.02),
        "attn_w_o": normal(ks[11], (N_ATTN_LAYERS, D_MODEL, D_MODEL), D_MODEL ** -0.5),
        "fourier_w_o": normal(ks[12], (N_FOURIER_LAYERS, D_MODEL, D_MODEL), D_MODEL ** -0.5),
        "mlp_w1": normal(ks[13], (DEPTH, D_MODEL, D_FF), D_MODEL ** -0.5),
        "mlp_w2": normal(ks[14], (DEPTH, D_FF, D_MODEL), D_FF ** -0.5),
        "final_norm_g": 1.0 + normal(ks[15], (D_MODEL,), 0.02),
    }

def reference(x, c, ctx, c_ctx, ada_w, ada_b, norm_mix_g, norm_mlp_g, attn_w_qkv, attn_q_norm_g,
              attn_k_norm_g, attn_w_o, fourier_w_o, mlp_w1, mlp_w2, final_norm_g):
    cos, sin = axial_rope_angles(x.shape[1])
    silu_c = jax.nn.silu(c)
    silu_cc = jax.nn.silu(c_ctx)
    for i in range(DEPTH):
        mixer = i % N_MIXERS
        j = i // N_MIXERS
        ctx_read_later = any(l % N_MIXERS == 0 for l in range(i + 1, DEPTH))
        mod_lat = (silu_c @ ada_w[i] + ada_b[i])[:, None, :]
        sh1, sc1, g1, sh2, sc2, g2 = jnp.split(mod_lat, N_MOD, axis=-1)
        mod_ctx = silu_cc @ ada_w[i] + ada_b[i]
        csh1, csc1, cg1, csh2, csc2, cg2 = jnp.split(mod_ctx, N_MOD, axis=-1)

        h_lat = modulate(rms_norm(x, norm_mix_g[i]), sh1, sc1)
        if mixer == 0 or ctx_read_later:
            h_ctx = modulate(rms_norm(ctx, norm_mix_g[i]), csh1, csc1)

        if mixer == 0:
            q_l, k_l, v_l = project_qkv(h_lat, attn_w_qkv[j], attn_q_norm_g[j], attn_k_norm_g[j])
            q_l = apply_rope(q_l, cos, sin)
            k_l = apply_rope(k_l, cos, sin)
            if ctx_read_later:
                q_c, k_c, v_c = project_qkv(h_ctx, attn_w_qkv[j], attn_q_norm_g[j], attn_k_norm_g[j])
                o_ctx = context_attention(q_c, k_c, v_c) @ attn_w_o[j]
            else:
                k_c, v_c = project_kv(h_ctx, attn_w_qkv[j][:, D_MODEL:], attn_k_norm_g[j])
            o_lat = latent_attention(q_l, k_l, v_l, k_c, v_c) @ attn_w_o[j]
        else:
            o_lat = fourier_mix(h_lat, fourier_w_o[j])
            if ctx_read_later:
                o_ctx = fourier_mix(h_ctx, fourier_w_o[j])

        x = x + g1 * o_lat
        x = x + g2 * sq_relu_mlp(modulate(rms_norm(x, norm_mlp_g[i]), sh2, sc2), mlp_w1[i], mlp_w2[i])
        if ctx_read_later:
            ctx = ctx + cg1 * o_ctx
            ctx = ctx + cg2 * sq_relu_mlp(modulate(rms_norm(ctx, norm_mlp_g[i]), csh2, csc2),
                                          mlp_w1[i], mlp_w2[i])
    return rms_norm(x, final_norm_g)


_drawn_inputs = setup_inputs


def setup_inputs(seed=0):
    import zlib

    import numpy as np

    out = dict(_drawn_inputs(seed))
    spreads = {}
    factors = {'norm_mix_g': 8.0,
     'norm_mlp_g': 2.786,
     'attn_q_norm_g': 8.0,
     'attn_k_norm_g': 8.0,
     'final_norm_g': 2.774}
    for name, (base, spread) in spreads.items():
        noise = np.random.default_rng([zlib.crc32(name.encode()), seed]).standard_normal(out[name].shape)
        drawn = base * np.exp(spread * noise) if base else spread * noise
        out[name] = __import__('jax').numpy.asarray(drawn.astype(out[name].dtype))
    for name, factor in factors.items():
        out[name] = (out[name] * factor).astype(out[name].dtype)
    return out
```

```python
from contextlib import ExitStack

import numpy as np

import concourse.bass as bass
from concourse import mybir

F32 = mybir.dt.float32
F32R = mybir.dt.float32r
ALU = mybir.AluOpType
ACT = mybir.ActivationFunctionType
AX_X = mybir.AxisListType.X

P = 128
D = 2048
KT = D // P
T = 256
HEADS, KV_HEADS, HD = 16, 4, 128
D_FF = 8192
FT = D_FF // P
GRID_W = 64
EPS = 1e-6
ROOT_D = float(D) ** 0.5
ROOT_HD = float(HD) ** 0.5
SCALE = float(HD) ** -0.5

NC = 1024
RAW = 4
SPLIT = 4
LOOKAHEAD = 4
START = 2 * KT

P_KV = START
P_Q = P_KV + 8
P_WO = (P_Q + 16, P_Q + 160)
P_UP = (P_WO[0] + 16, P_WO[1] + 16)
P_DOWN = (P_UP[0] + 64, P_UP[1] + 64)
N_PIECES = P_DOWN[1] + 64
LAST_SLICE = 2 * N_PIECES

SUMS = [(0, 2), (0, 3), (0, 4), (1, 0), (1, 1), (1, 2), (1, 3), (0, 5), (1, 4), (1, 5)]

V_C, V_CC, V_MIX, V_MLP, V_FIN, V_QG, V_KG = 0, 16, 32, 64, 96, 112, 113
N_MISC = 114


def layer_block(nc, x, c, ctx_in, c_ctx, ada_w, ada_b, norm_mix_g, norm_mlp_g, w_qkv, q_g, k_g, w_o,
                fourier_w, w1, w2, final_g, ident_in, swap_in, rope_in, dft_in, out):
    stack = ExitStack()
    base = [(nc.sbuf_base + 31) // 32 * 32]

    def place(name, shape, dt, at):
        return nc.alloc_sbuf_tensor_at(name, shape, dt, offset=at)

    def sb(name, shape, dt=F32):
        at = base[0]
        base[0] += (int(np.prod(shape[1:])) * 4 + 31) // 32 * 32
        return place(name, shape, dt, at)

    xT = sb("xT", [P, KT, T])
    h_hi = sb("h_hi", [P, KT, T], F32R)
    h_lo = sb("h_lo", [P, KT, T], F32R)
    shared = base[0]
    base[0] += 65536
    raw = sb("raw", [P, RAW, 2, NC])
    w_hi = sb("w_hi", [P, SPLIT, NC], F32R)
    w_lo = sb("w_lo", [P, SPLIT, NC], F32R)
    ada_raw = sb("ada_raw", [P, 2, D])
    base_ada_sum = base[0]
    ada_sum = sb("ada_sum", [P, D])
    ident = sb("ident", [P, P])
    ones = sb("ones", [P, P])
    swap = sb("swap", [P, P])
    bias_col = sb("bias_col", [P, 192])
    mod_col = sb("mod_col", [P, 192])
    misc = sb("misc", [P, N_MISC])
    silu = sb("silu", [P, KT, 2])
    sig = sb("sig", [P, 32])
    start_sum = sb("start_sum", [P, 2 * KT, 2])
    mod_sum = sb("mod_sum", [P, KT])
    tick = sb("tick", [P, 4])
    modc_col = sb("modc_col", [P, 32])
    a_col = sb("a_col", [P, 6, KT])
    rstd = sb("rstd", [P, 2, T])
    assert base[0] <= nc.sbuf_usable_end, base[0]

    x_rows = place("x_rows", [P, 2, D], F32, shared)
    c_rows = place("c_rows", [P, 2, D], F32, shared + 16384)
    ctxT = place("ctxT", [P, KT, T], F32, shared + 32768)
    vec_rows = place("vec_rows", [P, 3, P], F32, shared + 59392)
    start_rows = place("start_rows", [4, 2 * D], F32, shared)
    silu4 = place("silu4", [P, KT, P], F32R, base_ada_sum)
    sq = place("sq", [P, 2, 2, T], F32, shared + 49152)
    tn = place("tn", [P, 2, 2, T], F32, shared + 53248)
    hc_hi = place("hc_hi", [P, KT, T], F32R, shared)
    hc_lo = place("hc_lo", [P, KT, T], F32R, shared + 16384)
    qT = place("qT", [P, HEADS, T], F32, shared)
    prob = place("prob", [P, 3, 2 * T], F32, shared + 16384)
    probT = place("probT", [P, 2, 4, T], F32, shared + 22528)
    kT = place("kT", [P, KV_HEADS, 2 * T], F32, shared + 32768)
    vS = place("vS", [P, 4, KV_HEADS * HD], F32, shared + 40960)
    hsq = place("hsq", [P, 2, 2 * T], F32, shared + 49152)
    hrs = place("hrs", [P, 2 * T], F32, shared + 53248)
    hrot = place("hrot", [P, 2 * T], F32, shared + 55296)
    rope = place("rope", [P, 2, T], F32, shared + 57344)
    nmax = place("nmax", [P, 32, 4], F32, shared + 60928)
    u = place("u", [P, FT, T], F32, shared)
    z_hi = place("z_hi", [P, 2, 2, 2 * T], F32R, shared)
    z_lo = place("z_lo", [P, 2, 2, 2 * T], F32R, shared + 8192)
    dft = place("dft", [P, 2, 3 * T], F32, shared + 16384)
    dft_hi = place("dft_hi", [P, 2, 3 * T], F32R, shared + 22528)
    dft_lo = place("dft_lo", [P, 2, 3 * T], F32R, shared + 28672)
    yT = place("yT", [P, KT, T], F32, shared)
    y_rows = place("y_rows", [P, 2, D], F32, shared + 16384)

    ps = stack.enter_context(nc.psum_tensor("ps", [P, 8, 512], F32))

    def sem(name):
        return stack.enter_context(nc.semaphore(name))

    raw_in = [sem(f"raw_in{i}") for i in range(RAW)]
    ada_in = [sem(f"ada_in{i}") for i in range(2)]
    small_in = sem("small_in")
    x_in = sem("x_in")
    ctx_rows_in = sem("ctx_rows_in")
    dft_in_sem = sem("dft_in_sem")
    ones_set = sem("ones_set")
    silu4_zero = sem("silu4_zero")
    silu4_ready = sem("silu4_ready")
    start_out = sem("start_out")
    start_T = sem("start_T")
    modT_ready = sem("modT_ready")
    mod_part = sem("mod_part")
    hi_ready = sem("hi_ready")
    lo_ready = sem("lo_ready")
    slice_done = sem("slice_done")
    ada_used = sem("ada_used")
    mod_ready = sem("mod_ready")
    vec_T = sem("vec_T")
    vec_ready = sem("vec_ready")
    sig_ready = sem("sig_ready")
    silu_ready = sem("silu_ready")
    start_mods = sem("start_mods")
    a_ready = sem("a_ready")
    rows_T = sem("rows_T")
    rows_out = sem("rows_out")
    sq_ready = sem("sq_ready")
    sq_used = sem("sq_used")
    var_ready = sem("var_ready")
    rstd_ready = sem("rstd_ready")
    hvar_ready = sem("hvar_ready")
    hrs_ready = sem("hrs_ready")
    t_ready = sem("t_ready")
    mod_done = sem("mod_done")
    hhi_ready = sem("hhi_ready")
    h_ready = sem("h_ready")
    k_out = sem("k_out")
    v_out = sem("v_out")
    q_out = sem("q_out")
    hsq_ready = sem("hsq_ready")
    hss_ready = sem("hss_ready")
    dve_step = sem("dve_step")
    hnorm_ready = sem("hnorm_ready")
    hswap_ready = sem("hswap_ready")
    head_ready = sem("head_ready")
    score_ready = sem("score_ready")
    max_ready = sem("max_ready")
    exp_ready = sem("exp_ready")
    prob_ready = sem("prob_ready")
    probT_ready = sem("probT_ready")
    probT_out = sem("probT_out")
    pv_ready = sem("pv_ready")
    o_hi_ready = sem("o_hi_ready")
    o_ready = sem("o_ready")
    x_added = sem("x_added")
    relu_ready = sem("relu_ready")
    u_ready = sem("u_ready")
    held = sem("held")
    ticked = sem("ticked")
    uhi_ready = sem("uhi_ready")
    ulo_ready = sem("ulo_ready")
    dft_hi_ready = sem("dft_hi_ready")
    dft_ready = sem("dft_ready")
    z_mm = sem("z_mm")
    zhi_ready = sem("zhi_ready")
    z_ready = sem("z_ready")
    y_mm = sem("y_mm")
    yhi_ready = sem("yhi_ready")
    y_ready = sem("y_ready")
    fin_ready = sem("fin_ready")
    fin_T = sem("fin_T")
    fin_out = sem("fin_out")
    out_done = sem("out_done")

    wqkv_v = w_qkv[0].rearrange("(q k p) n -> q p k n", p=P, k=2)
    wo_v = (w_o[0].rearrange("(q k p) n -> q p k n", p=P, k=2),
            fourier_w[0].rearrange("(q k p) n -> q p k n", p=P, k=2))
    w1_v = [w1[l].rearrange("(q k p) (i b n) -> i b q p k n", p=P, k=2, b=2, n=NC) for l in range(2)]
    w2_v = [w2[l].rearrange("(g q k p) n -> g q p k n", p=P, k=2, q=4) for l in range(2)]
    ada_v = [ada_w[l].rearrange("(t p) (m n) -> m t p n", p=P, n=D) for l in range(2)]

    block = stack.enter_context(nc.Block())

    @block.sync
    def _(sp):
        def load_piece(piece, src, it=None, stride=0):
            if it is None:
                if piece >= RAW:
                    sp.wait_ge(lo_ready, 2 * (piece - RAW) + 2)
            else:
                sp.wait_ge(lo_ready, 2 * stride * it + (2 * (piece - RAW) + 2))
            sp.dma_start(raw[:, piece % RAW, :, :], src).then_inc(raw_in[piece % RAW], 16)

        for n in range(START):
            load_piece(n, ada_v[0][n // KT, n % KT].rearrange("p (k n) -> p k n", k=2))
        for q in range(8):
            load_piece(P_KV + q, wqkv_v[q, :, :, D:D + NC])
        for b in range(2):
            for q in range(8):
                load_piece(P_Q + 8 * b + q, wqkv_v[q, :, :, b * NC:(b + 1) * NC])
        for l in range(2):
            for b in range(2):
                for q in range(8):
                    load_piece(P_WO[l] + 8 * b + q, wo_v[l][q, :, :, b * NC:(b + 1) * NC])
            with sp.Fori(0, 4) as it:
                for b in range(2):
                    for q in range(8):
                        load_piece(P_UP[l] + 8 * b + q, w1_v[l][it, b, q], it, 16)
            for s in range(2):
                with sp.Fori(0, 8) as g:
                    for i in range(4):
                        load_piece(P_DOWN[l] + 32 * s + i, w2_v[l][g, i, :, :, s * NC:(s + 1) * NC], g, 4)
        sp.wait_ge(out_done, 32)

    @block.gpsimd
    def _(pool):
        def load_ada(n, src):
            if n >= 2:
                pool.wait_ge(ada_used, n - 1)
            pool.dma_start(ada_raw[:, n % 2, :], src).then_inc(ada_in[n % 2], 16)

        def load_ada_in_loop(n, src, it, stride, ticks):
            pool.wait_ge(ticked, it * stride + ticks)
            pool.wait_ge(ada_used, it * stride + (n - 1))
            nc.gpsimd.tensor_tensor(tick[:, 0:1], tick[:, 1:2], tick[:, 1:2], ALU.add).then_inc(ticked, 1)
            pool.dma_start(ada_raw[:, n % 2, :], src).then_inc(ada_in[n % 2], 16)

        nc.gpsimd.memset(tick[:, 0:2], 0.0).then_inc(ticked, 1)
        for i in range(3):
            for t in range(KT):
                load_ada(16 * i + t, ada_v[0][SUMS[i][1], t])
        with pool.Fori(0, 4) as it:
            for t in range(KT):
                load_ada_in_loop(48 + t, ada_v[1][it, t], it, 16, t + 1)
        for s in range(2):
            lay, m = SUMS[7 + s]
            with pool.Fori(0, 8) as g:
                src = ada_w[lay, :, m * D:(m + 1) * D].rearrange("(g a p) n -> g a p n", a=2, p=P)
                for a in range(2):
                    load_ada_in_loop(16 * (7 + s) + a, src[g, a], g, 2, 64 + 16 * s + a + 1)
        for t in range(KT):
            load_ada(16 * 9 + t, ada_v[1][SUMS[9][1], t])

    @block.scalar
    def _(act):
        def split_hi(s, it=None, stride=0):
            piece = s // 2
            if it is None:
                act.wait_ge(raw_in[piece % RAW], 16 * (piece // RAW + 1))
                if s >= SPLIT:
                    act.wait_ge(slice_done, s - SPLIT + 1)
            else:
                act.wait_ge(raw_in[piece % RAW], it * (stride // 2 // RAW * 16) + 16 * (piece // RAW + 1))
                act.wait_ge(slice_done, it * stride + (s - SPLIT + 1))
            act.activation(w_hi[:, s % SPLIT, :], raw[:, piece % RAW, s % 2, :], ACT.Copy).then_inc(hi_ready, 1)

        def hold(wait_sem, value, held_before):
            act.wait_ge(held, held_before)
            act.wait_ge(wait_sem, value)
            act.activation(sig[:, 0:1], sig[:, 1:2], ACT.Copy).then_inc(held, 1)

        def split_block(first, hook=None, it=None, stride=0, pieces=8):
            for p in range(pieces):
                if hook:
                    hook(p)
                for s in (first + 2 * p + LOOKAHEAD, first + 2 * p + 1 + LOOKAHEAD):
                    if it is not None or s < LAST_SLICE:
                        split_hi(s, it, stride)

        def square_pair(n, i, src):
            if 8 * n + i >= 2:
                act.wait_ge(sq_used, 8 * n + i - 1)
            act.activation(sq[:, i % 2], src[:, 2 * i:2 * i + 2, :], ACT.Square).then_inc(sq_ready, 1)

        def root(n, slot):
            act.wait_ge(var_ready, n + 1)
            act.activation(rstd[:, slot, :], rstd[:, slot, :], ACT.Sqrt).then_inc(rstd_ready, 1)

        def modulate(n, i, shift, dst):
            act.wait_ge(t_ready, 8 * n + i + 1)
            for k in range(2):
                kt = 2 * i + k
                act.activation(tn[:, i % 2, k], tn[:, i % 2, k], ACT.Identity, bias=shift[:, kt:kt + 1],
                               scale=a_col[:, n, kt:kt + 1]).then_inc(mod_done, 1)
            act.wait_ge(mod_done, 2 * (8 * n + i + 1))
            act.activation(dst[:, 2 * i:2 * i + 2, :], tn[:, i % 2], ACT.Copy).then_inc(hhi_ready, 1)

        act.wait_ge(ticked, 1)
        act.activation(tick[:, 2:3], tick[:, 1:2], ACT.Copy).then_inc(held, 1)
        act.activation(tick[:, 3:4], tick[:, 1:2], ACT.Copy).then_inc(u_ready, 1)
        act.dma_start(vec_rows[0:96, 0, :], ada_b[0].rearrange("(t p) -> t p", p=P)).then_inc(small_in, 16)
        act.dma_start(vec_rows[0:96, 1, :], ada_b[1].rearrange("(t p) -> t p", p=P)).then_inc(small_in, 16)
        for r, n, v in ((V_C, 16, c[0]), (V_CC, 16, c_ctx), (V_FIN, 16, final_g), (V_QG, 1, q_g[0]), (V_KG, 1, k_g[0])):
            act.dma_start(vec_rows[r:r + n, 2, :], v.rearrange("(t p) -> t p", p=P)).then_inc(small_in, 16)
        act.dma_start(vec_rows[V_MIX:V_MIX + 32, 2, :], norm_mix_g.rearrange("l (t p) -> (l t) p", p=P)).then_inc(small_in, 16)
        act.dma_start(vec_rows[V_MLP:V_MLP + 32, 2, :], norm_mlp_g.rearrange("l (t p) -> (l t) p", p=P)).then_inc(small_in, 16)
        act.dma_start(ident[:, :], ident_in).then_inc(small_in, 16)
        act.dma_start(swap[:, :], swap_in).then_inc(small_in, 16)
        act.dma_start(rope[:, :, :], rope_in.rearrange("a p t -> p a t")).then_inc(small_in, 16)
        act.dma_start(x_rows[:, :, :], x[0].rearrange("(a p) d -> p a d", p=P)).then_inc(x_in, 16)
        act.dma_start(c_rows[:, :, :], ctx_in[0].rearrange("(a p) d -> p a d", p=P)).then_inc(ctx_rows_in, 16)
        act.wait_ge(vec_ready, 3)
        act.activation(sig[:, :], misc[:, 0:32], ACT.Sigmoid).then_inc(sig_ready, 1)
        act.wait_ge(silu_ready, 1)
        act.wait_ge(silu4_zero, 1)
        act.activation(silu4[:, :, 0:4:2], silu[:, :, :], ACT.Copy).then_inc(silu4_ready, 1)

        def start_rows_out(m):
            act.wait_ge(slice_done, 32 * (m + 1))
            act.activation(start_rows[:, m * D:(m + 1) * D], ps[0:4, 4:8, :].rearrange("p b n -> p (b n)"),
                           ACT.Copy).then_inc(start_out, 1)

        def start_hook(n):
            if n == 16:
                act.wait_ge(rows_T, 16)
                start_rows_out(0)
            if n >= 16:
                st = (n - 16) // 8
                if n % 8 == 0:
                    act.wait_ge(rows_out, 8 * st + 8)
                square_pair(st, n % 8, (xT, ctxT)[st])

        for s in range(LOOKAHEAD):
            split_hi(s)
        split_block(0, start_hook, pieces=START)
        start_rows_out(1)
        root(0, 0)
        root(1, 1)

        def both(i):
            for n, dst, shift in ((0, h_hi, mod_col), (1, hc_hi, modc_col)):
                c0 = 2 * i + n
                act.wait_ge(t_ready, c0 + 1)
                for k in range(2):
                    kt = 2 * i + k
                    act.activation(tn[:, n, k], tn[:, n, k], ACT.Identity, bias=shift[:, kt:kt + 1],
                                   scale=a_col[:, n, kt:kt + 1]).then_inc(mod_done, 1)
                act.wait_ge(mod_done, 2 * (c0 + 1))
                act.activation(dst[:, 2 * i:2 * i + 2, :], tn[:, n], ACT.Copy).then_inc(hhi_ready, 1)

        act.wait_ge(a_ready, 2)
        both(0)
        split_block(2 * P_KV, lambda p: both(p + 1) if p < 7 else None)
        act.wait_ge(slice_done, 2 * P_Q)
        for g in range(KV_HEADS):
            act.activation(kT[:, g, :], ps[:, g, :], ACT.Copy).then_inc(k_out, 1)

        def head_src(r):
            return kT[:, r, :] if r < 4 else qT[:, 2 * (r - 4):2 * (r - 4) + 2, :].rearrange("p a t -> p (a t)")

        def head_square(r):
            if r < 4:
                act.wait_ge(k_out, 4)
            else:
                act.wait_ge(q_out, 4 if r < 8 else 8)
            if r >= 2:
                act.wait_ge(hss_ready, r - 1)
            act.activation(hsq[:, r % 2, :], head_src(r), ACT.Square).then_inc(hsq_ready, 1)

        def head_root(r):
            act.wait_ge(hvar_ready, r + 1)
            act.activation(hrs[:, :], hrs[:, :], ACT.Sqrt).then_inc(hrs_ready, 1)

        def head_hook(r0):
            return lambda p: head_square(r0 + p // 2) if p % 2 == 0 else head_root(r0 + p // 2)

        split_block(2 * P_Q, head_hook(0))
        for b in range(2):
            act.wait_ge(slice_done, 2 * P_Q + 16 * (b + 1))
            for i in range(4):
                act.activation(qT[:, 8 * b + 2 * i:8 * b + 2 * i + 2, :].rearrange("p a t -> p (a t)"),
                               ps[:, 4 * b + i, :], ACT.Copy).then_inc(q_out, 1)
            if b == 0:
                split_block(2 * P_Q + 16, head_hook(4))
        for r in range(8, 12):
            head_square(r)
            head_root(r)

        for n in range(37):
            if n < 32:
                act.wait_ge(max_ready, n + 1)
                if n >= 3:
                    act.wait_ge(probT_ready, n - 2)
                act.activation(prob[:, n % 3, :], ps[:, n % 3, :], ACT.Exp, bias=nmax[:, n, 1:2], scale=SCALE,
                               accum_out=nmax[:, n, 2:3]).then_inc(exp_ready, 1)
            m = n - 2
            if 0 <= m < 32:
                h, qt = m // 2, m % 2
                act.wait_ge(probT_ready, m + 1)
                if h >= 2:
                    act.wait_ge(pv_ready, h - 1)
                act.activation(probT[:, h % 2, :, qt * P:(qt + 1) * P],
                               ps[:, 3 + m % 2, :].rearrange("p (s q) -> p s q", s=4), ACT.Copy).then_inc(probT_out, 1)
            if n >= 5 and n % 2 == 1:
                h = (n - 5) // 2
                act.wait_ge(pv_ready, h + 1)
                act.activation(h_hi[:, h, :], ps[:, 5 + h % 2, 0:T], ACT.Copy).then_inc(o_hi_ready, 1)

        for l in range(2):
            n = 2 + 2 * l
            if l == 1:
                act.wait_ge(slice_done, 2 * P_WO[1])
                act.wait_ge(ulo_ready, 64)
                act.dma_start(dft[:, :, :], dft_in.rearrange("(k p) n -> p k n", p=P)).then_inc(dft_in_sem, 16)
                act.wait_ge(x_added, 32)
                for i in range(8):
                    square_pair(3, i, xT)
                root(3, 0)
                act.wait_ge(dft_in_sem, 16)
                act.activation(dft_hi[:, :, :], dft[:, :, :], ACT.Copy).then_inc(dft_hi_ready, 1)
                act.wait_ge(a_ready, 4)
                for i in range(2):
                    modulate(3, i, mod_col[:, 96:112], h_hi)
                for g in range(9):
                    if g < 8:
                        for nt in range(2):
                            act.wait_ge(z_mm, 2 * g + nt + 1)
                            if g >= 2:
                                act.wait_ge(y_mm, g - 1)
                            act.activation(z_hi[:, g % 2, nt, :], ps[:, 2 * (g % 2) + nt, :], ACT.Copy).then_inc(zhi_ready, 1)
                    if g + 2 < 8:
                        modulate(3, g + 2, mod_col[:, 96:112], h_hi)
                    if g >= 1:
                        act.wait_ge(y_mm, g)
                        act.activation(h_hi[:, 2 * g - 2:2 * g, :].rearrange("p a t -> p (a t)"), ps[:, 4 + (g - 1) % 2, :],
                                       ACT.Copy, scale=1.0 / T).then_inc(yhi_ready, 1)
            split_block(2 * P_WO[l])
            split_block(2 * P_WO[l] + 16)
            act.wait_ge(x_added, 16 + 32 * l)
            for i in range(8):
                square_pair(n, i, xT)
            root(n, 0)
            act.wait_ge(a_ready, n + 1)
            shift = mod_col[:, 96 * l + 48:96 * l + 64]
            modulate(n, 0, shift, h_hi)

            def relu_square(blk, it=None):
                b = blk % 2
                count = 32 * l + 4 * blk
                if it is None:
                    act.wait_ge(slice_done, 2 * P_UP[l] + 16 * (blk + 1))
                    f0 = 8 * blk
                    rows = u[:, f0:f0 + 8, :]
                else:
                    hold(slice_done, it * 32 + (2 * P_UP[l] + 16 * (blk + 1)), it * 4 + (12 * l - 3 + 2 * b))
                    rows = u[:, bass.ds(it * 16 + 8 * blk, 8), :]
                for j in range(4):
                    act.activation(rows[:, 2 * j:2 * j + 2, :], ps[:, 4 * b + j, :].rearrange("p (a t) -> p a t", a=2),
                                   ACT.Relu).then_inc(relu_ready, 1)
                if it is None:
                    act.wait_ge(relu_ready, count + 4)
                else:
                    hold(relu_ready, it * 8 + (count + 4), it * 4 + (12 * l - 3 + 2 * b + 1))
                act.activation(rows, rows, ACT.Square).then_inc(u_ready, 1)

            split_block(2 * P_UP[l], lambda p: modulate(n, p + 1, shift, h_hi) if p < 7 else None)
            relu_square(0)
            split_block(2 * P_UP[l] + 16)
            relu_square(1)
            with act.Fori(1, 4) as it:
                for b in range(2):
                    split_block(2 * P_UP[l] + 16 * b, None, it, 32)
                    relu_square(b, it)

            def u_hi(s, i, g=None):
                slot = i % 4
                if g is None:
                    src = u[:, 2 * i:2 * i + 2, :]
                else:
                    src = u[:, bass.ds(g * 8 + 2 * i, 2), :]
                act.activation(h_hi[:, 2 * slot:2 * slot + 2, :], src, ACT.Copy).then_inc(uhi_ready, 1)

            for s in range(2):
                first = 2 * P_DOWN[l] + 64 * s
                if s == 0:
                    act.wait_ge(slice_done, first)
                    act.wait_ge(u_ready, 8 * (l + 1) + 1)
                    u_hi(0, 0)
                for p in range(4):
                    u_hi(s, p + 1)
                    for q in (0, 1):
                        split_hi(first + 2 * p + q + LOOKAHEAD)
                with act.Fori(1, 7) as g:
                    for p in range(4):
                        u_hi(s, p + 1, g)
                        for q in (0, 1):
                            split_hi(first + 2 * p + q + LOOKAHEAD, g, 8)
                for p in range(28, 32):
                    if p < 31:
                        u_hi(s, p + 1)
                    elif s == 0:
                        u_hi(1, 0)
                    for q in (0, 1):
                        if first + 2 * p + q + LOOKAHEAD < LAST_SLICE:
                            split_hi(first + 2 * p + q + LOOKAHEAD)
        act.wait_ge(x_added, 64)
        for i in range(8):
            square_pair(5, i, xT)
        root(5, 0)
        for i in range(8):
            act.wait_ge(t_ready, 40 + i + 1)
            for k in range(2):
                act.activation(yT[:, 2 * i + k, :], tn[:, i % 2, k], ACT.Copy,
                               scale=a_col[:, 5, 2 * i + k:2 * i + k + 1]).then_inc(fin_ready, 1)
        for tt in range(2):
            act.wait_ge(fin_out, 4 * tt + 4)
            act.dma_start(out[0, tt * P:(tt + 1) * P, :], y_rows[:, tt, :]).then_inc(out_done, 16)

    @block.vector
    def _(dve):
        def split_lo(s, it=None, stride=0):
            if it is None:
                dve.wait_ge(hi_ready, s + 1)
            else:
                dve.wait_ge(hi_ready, it * stride + (s + 1))
            nc.vector.tensor_tensor(w_lo[:, s % SPLIT, :], raw[:, s // 2 % RAW, s % 2, :],
                                    w_hi[:, s % SPLIT, :].bitcast(F32), ALU.subtract).then_inc(lo_ready, 1)

        def ada_step(n, first, t, it=None, stride=0):
            if it is None:
                dve.wait_ge(ada_in[n % 2], 16 * (n // 2 + 1))
                if n > 0:
                    dve.wait_ge(ada_used, n)
            else:
                dve.wait_ge(ada_in[n % 2], it * (8 * stride) + 16 * (n // 2 + 1))
                dve.wait_ge(ada_used, it * stride + n)
            if isinstance(t, int):
                col = silu[:, t, 0:1]
            else:
                col = silu[:, bass.ds(t, 1), 0:1].rearrange("p a b -> p (a b)")
            if first:
                ins = nc.vector.tensor_scalar(ada_sum[:, :], ada_raw[:, n % 2, :], col, None, ALU.mult)
            else:
                ins = nc.vector.scalar_tensor_tensor(ada_sum[:, :], ada_raw[:, n % 2, :], col, ada_sum[:, :],
                                                     ALU.mult, ALU.add)
            ins.then_inc(ada_used, 1)

        def take_mod(i, bank0, col, it=None):
            for b in range(4):
                if it is None:
                    dve.wait_ge(modT_ready, 4 * i + b + 1)
                else:
                    dve.wait_ge(modT_ready, it * 4 + (4 * i + b + 1))
                nc.vector.tensor_reduce(mod_sum[:, 4 * b:4 * b + 4], ps[:, bank0 + b, :].rearrange("p (f k) -> p f k", f=4),
                                        AX_X, ALU.add).then_inc(mod_part, 1)
            if it is None:
                dve.wait_ge(mod_part, 4 * i + 4)
                dst, bias = mod_col[:, col:col + 16], bias_col[:, col:col + 16]
            else:
                dve.wait_ge(mod_part, it * 4 + (4 * i + 4))
                dst, bias = mod_col[:, bass.ds(it * 16 + col, 16)], bias_col[:, bass.ds(it * 16 + col, 16)]
            nc.vector.tensor_tensor(dst, mod_sum[:, :], bias, ALU.add).then_inc(mod_ready, 1)

        def gain(n, g0, scale_cols, wait):
            dve.wait_ge(*wait)
            nc.vector.scalar_tensor_tensor(a_col[:, n, :], scale_cols, 1.0, misc[:, g0:g0 + KT], ALU.add,
                                           ALU.mult).then_inc(dve_step, 1)
            steps[0] += 1
            dve.wait_ge(dve_step, steps[0])
            nc.vector.tensor_scalar(a_col[:, n, :], a_col[:, n, :], ROOT_D, None, ALU.mult).then_inc(a_ready, 1)

        steps = [0]
        norms = [0]
        lowered = {}

        def step(ins):
            ins.then_inc(dve_step, 1)
            steps[0] += 1
            dve.wait_ge(dve_step, steps[0])

        def make_rstd(n, bank, slot):
            norms[0] = n + 1
            if n >= 2:
                dve.wait_ge(t_ready, 8 * n)
            dve.wait_ge(sq_used, 8 * n + 8)
            step(nc.vector.tensor_scalar(rstd[:, slot, :], ps[:, bank, 0:T], EPS * D, None, ALU.add))
            nc.vector.reciprocal(rstd[:, slot, :], rstd[:, slot, :]).then_inc(var_ready, 1)

        def normalise(i, src, slot, r):
            if slot in lowered:
                dve.wait_ge(h_ready, lowered[slot])
            dve.wait_ge(rstd_ready, norms[0])
            nc.vector.tensor_tensor(tn[:, slot], src[:, 2 * i:2 * i + 2, :],
                                    rstd[:, r:r + 1, :].to_broadcast([P, 2, T]), ALU.mult).then_inc(t_ready, 1)

        def lower(c0, i, slot, hi, lo):
            lowered[slot] = c0 + 1
            dve.wait_ge(hhi_ready, c0 + 1)
            nc.vector.tensor_tensor(lo[:, 2 * i:2 * i + 2, :], tn[:, slot],
                                    hi[:, 2 * i:2 * i + 2, :].bitcast(F32), ALU.subtract).then_inc(h_ready, 1)

        def split_block(first, hook=None, ada=None, it=None, stride=0, pieces=8):
            for p in range(pieces):
                if hook:
                    hook(p)
                if ada:
                    ada(p)
                for s in (first + 2 * p + LOOKAHEAD, first + 2 * p + 1 + LOOKAHEAD):
                    split_lo(s, it, stride)

        def add_gated(l, m, wait, bank0, tiles):
            dve.wait_ge(*wait)
            for j in range(8):
                kt = tiles + j
                ins = nc.vector.scalar_tensor_tensor(xT[:, kt, :], ps[:, bank0 + j // 2, (j % 2) * T:(j % 2 + 1) * T],
                                                     mod_col[:, 96 * l + 16 * m + kt:96 * l + 16 * m + kt + 1],
                                                     xT[:, kt, :], ALU.mult, ALU.add)
                ins.then_inc(x_added, 1)

        nc.vector.memset(silu4[:, :, :].bitcast(F32), 0.0).then_inc(silu4_zero, 1)
        nc.vector.memset(ones[:, :], 1.0).then_inc(ones_set, 1)
        for i, (dst, w) in enumerate(((bias_col[:, 0:96], 96), (bias_col[:, 96:192], 96), (misc[:, :], N_MISC))):
            dve.wait_ge(vec_T, 3)
            nc.vector.tensor_copy(dst, ps[:, 0, i * P:i * P + w]).then_inc(vec_ready, 1)
        dve.wait_ge(sig_ready, 1)
        nc.vector.tensor_tensor(silu[:, :, :], misc[:, 0:32].rearrange("p (a t) -> p t a", a=2),
                                sig[:, :].rearrange("p (a t) -> p t a", a=2), ALU.mult).then_inc(silu_ready, 1)
        dve.wait_ge(silu4_ready, 1)
        nc.vector.tensor_tensor(silu4[:, :, 1:4:2], silu[:, :, :], silu4[:, :, 0:4:2].bitcast(F32),
                                ALU.subtract).then_inc(silu4_ready, 1)

        def start_hook(n):
            if 2 <= n < 18:
                v = n - 2
                dst = (xT if v < 8 else ctxT)[:, 2 * (v % 8):2 * (v % 8) + 2, :].rearrange("p a t -> p (a t)")
                dve.wait_ge(rows_T, v + 1)
                nc.vector.tensor_copy(dst, ps[:, v % 2, :]).then_inc(rows_out, 1)

        for s in range(LOOKAHEAD):
            split_lo(s)
        split_block(0, start_hook, pieces=START)
        make_rstd(0, 2, 0)
        make_rstd(1, 3, 1)
        dve.wait_ge(start_T, 1)
        step(nc.vector.tensor_reduce(start_sum[:, :, :].rearrange("p f a -> p (f a)"),
                                     ps[:, 0, 0:P].rearrange("p (f h) -> p f h", h=2), AX_X, ALU.add))
        nc.vector.tensor_tensor(mod_col[:, 0:32], start_sum[:, :, 0], bias_col[:, 0:32], ALU.add).then_inc(start_mods, 1)
        nc.vector.tensor_tensor(modc_col[:, :], start_sum[:, :, 1], bias_col[:, 0:32], ALU.add).then_inc(start_mods, 1)
        gain(0, V_MIX, mod_col[:, 16:32], (start_mods, 2))
        gain(1, V_MIX, modc_col[:, 16:32], (start_mods, 2))

        def norm_both(i):
            for n, src in ((0, xT), (1, ctxT)):
                normalise(i, src, n, n)

        def lower_both(i):
            for n, hi, lo in ((0, h_hi, h_lo), (1, hc_hi, hc_lo)):
                lower(2 * i + n, i, n, hi, lo)

        norm_both(0)
        lower_both(0)

        def kv_hook(p):
            if p < 7:
                norm_both(p + 1)
                lower_both(p + 1)

        def kv_ada(p):
            for t in (2 * p, 2 * p + 1):
                ada_step(t, t == 0, t)

        split_block(2 * P_KV, kv_hook, kv_ada)
        dve.wait_ge(slice_done, 2 * P_Q)
        for st in range(4):
            nc.vector.tensor_copy(vS[:, st, :], ps[:, 4 + st, :]).then_inc(v_out, 1)
        take_mod(0, 4, 32)
        step(nc.vector.tensor_scalar(misc[:, V_QG:V_KG + 1], misc[:, V_QG:V_KG + 1], ROOT_HD, None, ALU.mult))

        def head_src(r):
            return kT[:, r, :] if r < 4 else qT[:, 2 * (r - 4):2 * (r - 4) + 2, :].rearrange("p a t -> p (a t)")

        def head_var(r, bank):
            dve.wait_ge(hss_ready, r + 1)
            if r:
                dve.wait_ge(hnorm_ready, r)
            step(nc.vector.tensor_scalar(hrs[:, :], ps[:, bank, :], EPS * HD, None, ALU.add))
            nc.vector.reciprocal(hrs[:, :], hrs[:, :]).then_inc(hvar_ready, 1)

        def head_norm(r):
            dve.wait_ge(hrs_ready, r + 1)
            g = V_KG if r < 4 else V_QG
            nc.vector.scalar_tensor_tensor(head_src(r), head_src(r), misc[:, g:g + 1], hrs[:, :], ALU.mult,
                                           ALU.mult).then_inc(hnorm_ready, 1)

        def head_rope(r, bank):
            heads = 1 if r < 4 else 2
            dve.wait_ge(hswap_ready, r + 1)
            dst = head_src(r)[:, 0:heads * T].rearrange("p (a t) -> p a t", a=heads)
            sw = ps[:, bank, 0:heads * T].rearrange("p (a t) -> p a t", a=heads)
            rot = hrot[:, 0:heads * T].rearrange("p (a t) -> p a t", a=heads)
            cos = rope[:, 0:1, :].to_broadcast([P, heads, T])
            sin = rope[:, 1:2, :].to_broadcast([P, heads, T])
            if r:
                dve.wait_ge(head_ready, r)
            step(nc.vector.tensor_tensor(rot, sw, sin, ALU.mult))
            step(nc.vector.tensor_tensor(dst, dst, cos, ALU.mult))
            nc.vector.tensor_tensor(dst, dst, rot, ALU.add).then_inc(head_ready, 1)

        def head_hook(r0, bank):
            def hook(p):
                if p % 2 == 0:
                    if p:
                        head_rope(r0 + p // 2 - 1, bank + 1)
                    head_var(r0 + p // 2, bank)
                else:
                    head_norm(r0 + p // 2)
            return hook

        for b in range(2):
            split_block(2 * P_Q + 16 * b, head_hook(4 * b, 5 if b == 0 else 1),
                        lambda p: ada_step(16 + 8 * b + p, b == 0 and p == 0, 8 * b + p))
            head_rope(4 * b + 3, 6 if b == 0 else 2)
        for r in range(8, 12):
            head_var(r, 1)
            head_norm(r)
            head_rope(r, 2)
        take_mod(1, 0, 48)

        for n in range(37):
            if n < 32:
                dve.wait_ge(score_ready, n + 1)
                step(nc.vector.tensor_reduce(nmax[:, n, 0:1], ps[:, n % 3, :], AX_X, ALU.max))
                nc.vector.tensor_scalar(nmax[:, n, 1:2], nmax[:, n, 0:1], -SCALE, None, ALU.mult).then_inc(max_ready, 1)
            m = n - 1
            if 0 <= m < 32:
                dve.wait_ge(exp_ready, m + 1)
                step(nc.vector.reciprocal(nmax[:, m, 3:4], nmax[:, m, 2:3]))
                nc.vector.tensor_scalar(prob[:, m % 3, :], prob[:, m % 3, :], nmax[:, m, 3:4], None,
                                        ALU.mult).then_inc(prob_ready, 1)
            if n >= 5 and n % 2 == 1:
                h = (n - 5) // 2
                dve.wait_ge(o_hi_ready, h + 1)
                nc.vector.tensor_tensor(h_lo[:, h, :], ps[:, 5 + h % 2, 0:T], h_hi[:, h, :].bitcast(F32),
                                        ALU.subtract).then_inc(o_ready, 1)

        for l in range(2):
            n = 2 + 2 * l
            if l == 1:
                gain(3, V_MIX + KT, mod_col[:, 96 + 16:96 + 32], (mod_ready, 9))
                make_rstd(3, 0, 0)
                dve.wait_ge(dft_hi_ready, 1)
                nc.vector.tensor_tensor(dft_lo[:, :, :], dft[:, :, :], dft_hi[:, :, :].bitcast(F32),
                                        ALU.subtract).then_inc(dft_ready, 1)
                normalise(0, xT, 0, 0)
                normalise(1, xT, 1, 0)
                for i in range(2):
                    lower(24 + i, i, i % 2, h_hi, h_lo)
                    normalise(i + 2, xT, i % 2, 0)
                for g in range(9):
                    if g < 8:
                        for nt in range(2):
                            dve.wait_ge(zhi_ready, 2 * g + nt + 1)
                            nc.vector.tensor_tensor(z_lo[:, g % 2, nt, :], ps[:, 2 * (g % 2) + nt, :],
                                                    z_hi[:, g % 2, nt, :].bitcast(F32), ALU.subtract).then_inc(z_ready, 1)
                    if g + 2 < 8:
                        lower(24 + g + 2, g + 2, g % 2, h_hi, h_lo)
                        if g + 4 < 8:
                            normalise(g + 4, xT, g % 2, 0)
                    if g >= 1:
                        dve.wait_ge(yhi_ready, g)
                        nc.vector.scalar_tensor_tensor(h_lo[:, 2 * g - 2:2 * g, :].rearrange("p a t -> p (a t)"),
                                                       ps[:, 4 + (g - 1) % 2, :], 1.0 / T,
                                                       h_hi[:, 2 * g - 2:2 * g, :].rearrange("p a t -> p (a t)").bitcast(F32),
                                                       ALU.mult, ALU.subtract).then_inc(y_ready, 1)
            s = 2 if l == 0 else 9
            for b in range(2):
                split_block(2 * P_WO[l] + 16 * b, None,
                            lambda p: ada_step(16 * s + 8 * b + p, b == 0 and p == 0, 8 * b + p))
                add_gated(l, 2, (slice_done, 2 * P_WO[l] + 16 * (b + 1)), 4 * b, 8 * b)
            lay, m = SUMS[s]
            take_mod(s, 0, 96 * lay + 16 * m)
            gain(n, V_MLP + KT * l, mod_col[:, 96 * l + 64:96 * l + 80], (mod_ready, s + 1))
            make_rstd(n, 0, 0)
            normalise(0, xT, 0, 0)
            normalise(1, xT, 1, 0)
            lower(8 * n, 0, 0, h_hi, h_lo)

            def feed(p):
                if p < 6:
                    normalise(p + 2, xT, p % 2, 0)
                if p < 7:
                    lower(8 * n + p + 1, p + 1, (p + 1) % 2, h_hi, h_lo)

            for b in range(2):
                split_block(2 * P_UP[l] + 16 * b, feed if b == 0 else None,
                            (lambda p: ada_step(48 + 8 * b + p, b == 0 and p == 0, 8 * b + p)) if l == 0 else None)
            if l == 0:
                take_mod(3, 0, 96)
            with dve.Fori(1, 4) as it:
                for b in range(2):
                    split_block(2 * P_UP[l] + 16 * b, None,
                                (lambda p: ada_step(48 + 8 * b + p, b == 0 and p == 0, 8 * b + p, it, 16)) if l == 0 else None,
                                it, 32)
                if l == 0:
                    take_mod(3, 0, 96, it)

            def u_lo(s, i, g=None):
                slot = i % 4
                if g is None:
                    dve.wait_ge(uhi_ready, 64 * l + 32 * s + i + 1)
                    src = u[:, 2 * i:2 * i + 2, :]
                else:
                    dve.wait_ge(uhi_ready, g * 4 + (64 * l + 32 * s + i + 1))
                    src = u[:, bass.ds(g * 8 + 2 * i, 2), :]
                nc.vector.tensor_tensor(h_lo[:, 2 * slot:2 * slot + 2, :], src,
                                        h_hi[:, 2 * slot:2 * slot + 2, :].bitcast(F32), ALU.subtract).then_inc(ulo_ready, 1)

            for s in range(2):
                first = 2 * P_DOWN[l] + 64 * s
                n0 = 16 * (7 + s)
                if s == 0:
                    u_lo(0, 0)
                for p in range(4):
                    u_lo(s, p + 1)
                    if l == 0 and p % 2 == 0:
                        ada_step(n0 + p // 2, p == 0, p // 2)
                    for q in (0, 1):
                        split_lo(first + 2 * p + q + LOOKAHEAD)
                with dve.Fori(1, 7) as g:
                    for p in range(4):
                        u_lo(s, p + 1, g)
                        if l == 0 and p % 2 == 0:
                            ada_step(n0 + p // 2, False, g * 2 + p // 2, g, 2)
                        for q in (0, 1):
                            split_lo(first + 2 * p + q + LOOKAHEAD, g, 8)
                for p in range(28, 32):
                    if p < 31:
                        u_lo(s, p + 1)
                    elif s == 0:
                        u_lo(1, 0)
                    if l == 0 and p % 2 == 0:
                        ada_step(n0 + p // 2, False, p // 2)
                    for q in (0, 1):
                        if first + 2 * p + q + LOOKAHEAD < LAST_SLICE:
                            split_lo(first + 2 * p + q + LOOKAHEAD)
                if l == 0:
                    lay, m = SUMS[7 + s]
                    take_mod(7 + s, 4 if s == 0 else 0, 96 * lay + 16 * m)
                    if s == 0:
                        dve.wait_ge(mod_ready, 8)
                add_gated(l, 5, (slice_done, first + 64), 4 * s, 8 * s)
        nc.vector.tensor_scalar(a_col[:, 5, :], misc[:, V_FIN:V_FIN + KT], ROOT_D, None, ALU.mult)
        make_rstd(5, 0, 0)
        for i in range(8):
            if i >= 2:
                dve.wait_ge(fin_ready, 2 * (i - 1))
            normalise(i, xT, i % 2, 0)
        for tt in range(2):
            for i in range(4):
                dve.wait_ge(fin_T, 4 * tt + i + 1)
                nc.vector.tensor_copy(y_rows[:, tt, 512 * i:512 * (i + 1)], ps[:, 1 + (4 * tt + i) % 4, :]).then_inc(fin_out, 1)

    @block.tensor
    def _(pe):
        mm = nc.tensor.matmul

        def three(dst, w_h, w_l, m_h, m_l, start, stop):
            mm(dst, w_h, m_h, start=start, stop=False, skip_group_check=True)
            mm(dst, w_h, m_l, start=False, stop=False, skip_group_check=True)
            return mm(dst, w_l, m_h, start=False, stop=stop, skip_group_check=True)

        def tile_out(bank0, j):
            return ps[:, bank0 + j // 2, (j % 2) * T:(j % 2 + 1) * T]

        def project_slice(s, bank0, rows, first, last, it=None, stride=0, before_bank=None):
            if it is None:
                pe.wait_ge(lo_ready, s + 1)
            else:
                pe.wait_ge(lo_ready, it * stride + (s + 1))
            for j in range(8):
                if j % 2 == 0 and before_bank:
                    before_bank(j // 2)
                w = slice(j * P, (j + 1) * P)
                ins = three(tile_out(bank0, j), w_hi[:, s % SPLIT, w], w_lo[:, s % SPLIT, w], h_hi[:, rows, :],
                            h_lo[:, rows, :], first and j % 2 == 0, last)
            ins.then_inc(slice_done, 1)

        def turn_ada(i, bank0, it=None):
            if it is None:
                pe.wait_ge(ada_used, 16 * (i + 1))
            else:
                pe.wait_ge(ada_used, it * 16 + 16 * (i + 1))
            for b in range(4):
                for f in range(4):
                    w = slice((4 * b + f) * P, (4 * b + f + 1) * P)
                    ins = nc.tensor.transpose(ps[:, bank0 + b, f * P:(f + 1) * P], ada_sum[:, w], ident[:, :])
                ins.then_inc(modT_ready, 1)

        def sum_pair(n, bank, i):
            pe.wait_ge(sq_ready, 8 * n + i + 1)
            for k in range(2):
                ins = mm(ps[:, bank, 0:T], ones[:, :], sq[:, i % 2, k, :], start=(i == 0 and k == 0), stop=(i == 7 and k == 1))
            ins.then_inc(sq_used, 1)

        def sum_squares(n, bank):
            for i in range(8):
                sum_pair(n, bank, i)

        pe.wait_ge(small_in, 16 * 12)
        for i, n in enumerate((96, 96, N_MISC)):
            nc.tensor.transpose(ps[:, 0, i * P:i * P + n], vec_rows[0:n, i, :], ident[0:n, 0:n]).then_inc(vec_T, 1)

        def turn_rows(v):
            if v == 0:
                pe.wait_ge(x_in, 16)
                pe.wait_ge(vec_ready, 3)
            if v == 8:
                pe.wait_ge(ctx_rows_in, 16)
            if v >= 2:
                pe.wait_ge(rows_out, v - 1)
            src = x_rows if v < 8 else c_rows
            for k in range(2):
                for tt in range(2):
                    f = 2 * (v % 8) + k
                    ins = nc.tensor.transpose(ps[:, v % 2, k * T + tt * P:k * T + (tt + 1) * P], src[:, tt, f * P:(f + 1) * P],
                                              ident[:, :])
            ins.then_inc(rows_T, 1)

        pe.wait_ge(silu4_ready, 2)
        pe.wait_ge(ones_set, 1)
        for n in range(START):
            m, t = n // KT, n % KT
            if n == KT:
                pe.wait_ge(start_out, 1)
            for k in range(2):
                s = 2 * n + k
                pe.wait_ge(lo_ready, s + 1)
                for h in range(2):
                    bank, cols = 4 + 2 * k + h, slice(512 * h, 512 * (h + 1))
                    mm(ps[:, bank, :], silu4[:, t, :], w_hi[:, s % SPLIT, cols], start=(t == 0), stop=False)
                    ins = mm(ps[:, bank, :], silu4[:, t, :], w_lo[:, s % SPLIT, cols], start=False, stop=(t == KT - 1))
                ins.then_inc(slice_done, 1)
            if n < 16:
                turn_rows(n)
            if n >= 16:
                sum_pair((n - 16) // 8, 2 + (n - 16) // 8, n % 8)
        pe.wait_ge(start_out, 2)
        for f in range(2 * KT):
            ins = nc.tensor.transpose(ps[:, 0, 4 * f:4 * f + 4], start_rows[:, f * P:(f + 1) * P], ident[0:4, 0:4])
        ins.then_inc(start_T, 1)

        for s in range(16):
            if s % 2 == 0:
                pe.wait_ge(h_ready, s + 2)
            pe.wait_ge(lo_ready, 2 * P_KV + s + 1)
            for j in range(4):
                w = slice(j * P, (j + 1) * P)
                for st, (hh, hl) in enumerate(((h_hi, h_lo), (hc_hi, hc_lo))):
                    three(ps[:, j, st * T:(st + 1) * T], w_hi[:, s % SPLIT, w], w_lo[:, s % SPLIT, w], hh[:, s, :], hl[:, s, :],
                          s == 0 and st == 0, s == 15)
            for st in range(4):
                hh, hl = (h_hi, h_lo) if st < 2 else (hc_hi, hc_lo)
                tok = slice((st % 2) * P, (st % 2 + 1) * P)
                ins = three(ps[:, 4 + st, :], hh[:, s, tok], hl[:, s, tok], w_hi[:, s % SPLIT, 512:1024],
                            w_lo[:, s % SPLIT, 512:1024], s == 0, s == 15)
            ins.then_inc(slice_done, 1)
        pe.wait_ge(v_out, 4)
        turn_ada(0, 4)

        def head_ss(r, bank):
            pe.wait_ge(hsq_ready, r + 1)
            if r >= 1:
                pe.wait_ge(hvar_ready, r)
            mm(ps[:, bank, :], ones[:, :], hsq[:, r % 2, :], start=True, stop=True).then_inc(hss_ready, 1)

        def head_swap(r, bank):
            pe.wait_ge(hnorm_ready, r + 1)
            if r >= 1:
                pe.wait_ge(head_ready, r)
            src = kT[:, r, :] if r < 4 else qT[:, 2 * (r - 4):2 * (r - 4) + 2, :].rearrange("p a t -> p (a t)")
            mm(ps[:, bank, :], swap[:, :], src, start=True, stop=True).then_inc(hswap_ready, 1)

        for b in range(2):
            for s in range(16):
                if s == 0 and b == 0:
                    pe.wait_ge(k_out, 4)
                if s == 0 and b == 1:
                    pe.wait_ge(head_ready, 4)
                if s % 4 == 1:
                    if s == 1 and b == 0:
                        pe.wait_ge(mod_part, 4)
                    if s == 1 and b == 1:
                        pe.wait_ge(q_out, 4)
                    head_ss(4 * b + s // 4, 5 if b == 0 else 1)
                if s % 4 == 3:
                    head_swap(4 * b + s // 4, 6 if b == 0 else 2)
                project_slice(2 * P_Q + 16 * b + s, 4 * b, s, s == 0, s == 15)
        for r in range(8, 12):
            if r == 8:
                pe.wait_ge(head_ready, 8)
            head_ss(r, 1)
            head_swap(r, 2)
        pe.wait_ge(head_ready, 12)
        turn_ada(1, 0)

        for n in range(36):
            if n < 32:
                h, qt = n // 2, n % 2
                if n == 0:
                    pe.wait_ge(head_ready, 12)
                    pe.wait_ge(q_out, 8)
                    pe.wait_ge(mod_part, 8)
                if n >= 3:
                    pe.wait_ge(exp_ready, n - 2)
                mm(ps[:, n % 3, :], qT[:, h, qt * P:(qt + 1) * P], kT[:, h // 4, :], start=True, stop=True).then_inc(score_ready, 1)
            m = n - 2
            if 0 <= m < 32:
                pe.wait_ge(prob_ready, m + 1)
                if m >= 2:
                    pe.wait_ge(probT_out, m - 1)
                for st in range(4):
                    ins = nc.tensor.transpose(ps[:, 3 + m % 2, st * P:(st + 1) * P], prob[:, m % 3, st * P:(st + 1) * P], ident[:, :])
                ins.then_inc(probT_ready, 1)
            if n >= 4 and n % 2 == 0:
                h = (n - 4) // 2
                pe.wait_ge(probT_out, 2 * h + 2)
                if h >= 2:
                    pe.wait_ge(o_ready, h - 1)
                g = h // 4
                for st in range(4):
                    ins = mm(ps[:, 5 + h % 2, 0:T], vS[:, st, g * HD:(g + 1) * HD], probT[:, h % 2, st, :], start=(st == 0), stop=(st == 3))
                ins.then_inc(pv_ready, 1)

        for l in range(2):
            n = 2 + 2 * l
            if l == 1:
                sum_squares(3, 0)

                def stage1(g):
                    pe.wait_ge(h_ready, 24 + g + 1)
                    if g >= 2:
                        pe.wait_ge(z_ready, 2 * g - 2)
                    for nt in range(2):
                        tok = slice(nt * P, (nt + 1) * P)
                        for k in range(2):
                            ins = three(ps[:, 2 * (g % 2) + nt, :], h_hi[:, 2 * g + k, tok], h_lo[:, 2 * g + k, tok],
                                        dft_hi[:, k, 0:2 * T], dft_lo[:, k, 0:2 * T], k == 0, k == 1)
                        ins.then_inc(z_mm, 1)

                def stage2(g):
                    pe.wait_ge(z_ready, 2 * g + 2)
                    if g >= 2:
                        pe.wait_ge(y_ready, g - 1)
                    for ct in range(2):
                        for cs in range(2):
                            for nt in range(2):
                                c0 = cs * T + ct * P
                                r0 = cs * 2 * T
                                ins = three(ps[:, 4 + g % 2, ct * T:(ct + 1) * T], z_hi[:, g % 2, nt, c0:c0 + P],
                                            z_lo[:, g % 2, nt, c0:c0 + P], dft_hi[:, nt, r0:r0 + T], dft_lo[:, nt, r0:r0 + T],
                                            ct == 0 and cs == 0 and nt == 0, cs == 1 and nt == 1)
                    ins.then_inc(y_mm, 1)

                pe.wait_ge(dft_ready, 1)
                pe.wait_ge(rstd_ready, 4)
                pe.wait_ge(mod_ready, 9)
                pe.wait_ge(x_added, 32)
                stage1(0)
                for g in range(8):
                    if g + 1 < 8:
                        stage1(g + 1)
                    stage2(g)
            for b in range(2):
                for s in range(16):
                    if l == 0:
                        if s == 0 and b == 0:
                            pe.wait_ge(probT_out, 32)
                            pe.wait_ge(exp_ready, 32)
                        if b == 0:
                            pe.wait_ge(o_ready, s + 1)
                    else:
                        if s == 0 and b == 0:
                            pe.wait_ge(z_ready, 16)
                        if b == 0:
                            pe.wait_ge(y_ready, s // 2 + 1)
                    project_slice(2 * P_WO[l] + 16 * b + s, 4 * b, s, s == 0, s == 15)
            pe.wait_ge(x_added, 8 + 32 * l)
            s0 = 2 if l == 0 else 9
            turn_ada(s0, 0)
            pe.wait_ge(x_added, 16 + 32 * l)
            pe.wait_ge(mod_part, 4 * s0 + 4)
            sum_squares(n, 0)
            pe.wait_ge(rstd_ready, n + 1)
            with pe.Fori(0, 4) as it:
                for b in range(2):
                    for s in range(16):
                        if s % 2 == 0:
                            pe.wait_ge(h_ready, 8 * n + s // 2 + 1)
                        hook = None
                        if s == 0 and b == 0 and l == 0:
                            def hook(bank):
                                pe.wait_ge(mod_part, it * 4 + (9 + bank))
                        project_slice(2 * P_UP[l] + 16 * b + s, 4 * b, s, s == 0, s == 15, it, 32, hook)
                    pe.wait_ge(u_ready, it * 2 + (8 * l + b + 1))
                if l == 0:
                    turn_ada(3, 0, it)
            for sw in range(2):
                first = 2 * P_DOWN[l] + 64 * sw

                def group(g, i0, head, tail):
                    for i in range(4):
                        piece = i0 + i
                        if g is None:
                            pe.wait_ge(ulo_ready, 64 * l + 32 * sw + piece + 1)
                        else:
                            pe.wait_ge(ulo_ready, g * 4 + (64 * l + 32 * sw + piece + 1))
                        for k in range(2):
                            hook = None
                            if head and i == 0 and k == 0 and l == 0:
                                def hook(bank):
                                    pe.wait_ge(mod_part, 4 * (6 + sw) + bank + 1)
                            project_slice(first + 2 * piece + k, 4 * sw, 2 * i + k, head and i == 0 and k == 0,
                                          tail and i == 3 and k == 1, g, 8, hook)

                pe.wait_ge(u_ready, 8 * l + 8 + sw)
                group(None, 0, True, False)
                with pe.Fori(1, 7) as g:
                    group(g, 0, False, False)
                group(None, 28, False, True)
                if l == 0:
                    if sw == 0:
                        pe.wait_ge(u_ready, 9)
                        turn_ada(7, 4)
                    else:
                        pe.wait_ge(x_added, 24)
                        turn_ada(8, 0)
            pe.wait_ge(x_added, 32 + 32 * l)
        sum_squares(5, 0)
        for tt in range(2):
            for i in range(4):
                v = 4 * tt + i
                if tt == 0:
                    pe.wait_ge(fin_ready, 4 * i + 4)
                if v >= 4:
                    pe.wait_ge(fin_out, v - 3)
                for k in range(4):
                    ins = nc.tensor.transpose(ps[:, 1 + v % 4, k * P:(k + 1) * P], yT[:, 4 * i + k, tt * P:(tt + 1) * P], ident[:, :])
                ins.then_inc(fin_T, 1)

    stack.close()


def constants():
    ident = np.eye(P, dtype=np.float32)
    swap = np.zeros((P, P), np.float32)
    for i in range(0, P, 2):
        swap[i + 1, i] = -1.0
        swap[i, i + 1] = 1.0
    n_freq = HD // 4
    inv = (np.float32(10000.0) ** (-np.arange(n_freq, dtype=np.float32) / np.float32(n_freq))).astype(np.float32)
    tok = np.arange(T)
    row, col = (tok // GRID_W).astype(np.float32), (tok % GRID_W).astype(np.float32)
    ang = np.concatenate([row[:, None] * inv, col[:, None] * inv], axis=1)
    ang = np.repeat(ang.T, 2, axis=0).astype(np.float64)
    rope = np.stack([np.cos(ang), np.sin(ang)]).astype(np.float32)
    k = np.outer(np.arange(T), np.arange(T)) % T
    th = 2.0 * np.pi * k / T
    dft = np.concatenate([np.cos(th), np.sin(th), -np.sin(th)], axis=1).astype(np.float32)
    return ident, swap, rope, dft


_INS = ["x", "c", "ctx", "c_ctx", "ada_w", "ada_b", "norm_mix_g", "norm_mlp_g", "attn_w_qkv", "attn_q_norm_g",
        "attn_k_norm_g", "attn_w_o", "fourier_w_o", "mlp_w1", "mlp_w2", "final_norm_g"]


def kernel(**inputs):
    import numpy as _np
    import concourse.bacc as _bacc
    from concourse import mybir as _mybir
    from concourse.bass_utils import run_bass_kernel_spmd as _run

    nc = _bacc.Bacc("TRN2", target_bir_lowering=False, num_devices=1)
    arrays, args = {}, []
    for name in _INS:
        a = _np.ascontiguousarray(inputs[name])
        arrays[f"in_{name}"] = a
        args.append(nc.dram_tensor(f"in_{name}", a.shape, _mybir.dt.from_np(a.dtype), kind="ExternalInput").ap())
    for name, a in zip(("ident", "swap", "rope", "dft"), constants()):
        arrays[f"const_{name}"] = a
        args.append(nc.dram_tensor(f"const_{name}", a.shape, _mybir.dt.from_np(a.dtype), kind="ExternalInput").ap())
    args.append(nc.dram_tensor("out_0", (1, T, D), _mybir.dt.float32, kind="ExternalOutput").ap())
    layer_block(nc, *args)
    r = _run(nc, [arrays], core_ids=[0])
    return r.results[0]["out_0"]
```

```python
from contextlib import ExitStack

import numpy as np

import concourse.bass as bass
from concourse import mybir

F32 = mybir.dt.float32
F32R = mybir.dt.float32r
ALU = mybir.AluOpType
ACT = mybir.ActivationFunctionType
AX_X = mybir.AxisListType.X

P = 128
D = 2048
KT = D // P
T = 256
HEADS, KV_HEADS, HD = 16, 4, 128
D_FF = 8192
FT = D_FF // P
GRID_W = 64
EPS = 1e-6
ROOT_D = float(D) ** 0.5
ROOT_HD = float(HD) ** 0.5
SCALE = float(HD) ** -0.5

NC = 1024
RAW = 4
SPLIT = 4
LOOKAHEAD = 4
START = 2 * KT

P_KV = START
P_Q = P_KV + 8
P_WO = (P_Q + 16, P_Q + 160)
P_UP = (P_WO[0] + 16, P_WO[1] + 16)
P_DOWN = (P_UP[0] + 64, P_UP[1] + 64)
N_PIECES = P_DOWN[1] + 64
LAST_SLICE = 2 * N_PIECES

SUMS = [(0, 2), (0, 3), (0, 4), (1, 0), (1, 1), (1, 2), (0, 5), (1, 3), (1, 4), (1, 5)]
HALVES = 4


def mods_ready(i):
    return i + 1 if i < HALVES else 2 * i - HALVES + 2 if i < HALVES + 2 else i + 3


V_C, V_CC, V_MIX, V_MLP, V_FIN, V_QG, V_KG = 0, 16, 32, 64, 96, 112, 113
N_MISC = 114


def layer_block(nc, x, c, ctx_in, c_ctx, ada_w, ada_b, norm_mix_g, norm_mlp_g, w_qkv, q_g, k_g, w_o,
                fourier_w, w1, w2, final_g, ident_in, swap_in, rope_in, dft_in, out):
    stack = ExitStack()
    base = [(nc.sbuf_base + 31) // 32 * 32]

    def place(name, shape, dt, at):
        return nc.alloc_sbuf_tensor_at(name, shape, dt, offset=at)

    def sb(name, shape, dt=F32):
        at = base[0]
        base[0] += (int(np.prod(shape[1:])) * 4 + 31) // 32 * 32
        return place(name, shape, dt, at)

    xT = sb("xT", [P, KT, T])
    h_hi = sb("h_hi", [P, KT, T], F32R)
    h_lo = sb("h_lo", [P, KT, T], F32R)
    shared = base[0]
    base[0] += 65536
    raw = sb("raw", [P, RAW, 2, NC])
    w_hi = sb("w_hi", [P, SPLIT, NC], F32R)
    w_lo = sb("w_lo", [P, SPLIT, NC], F32R)
    ada_raw = sb("ada_raw", [P, 2, D])
    base_ada_sum = base[0]
    ada_sum = sb("ada_sum", [P, D])
    ident = sb("ident", [P, P])
    ones = sb("ones", [P, P])
    swap = sb("swap", [P, P])
    bias_col = sb("bias_col", [P, 192])
    mod_col = sb("mod_col", [P, 192])
    misc = sb("misc", [P, N_MISC])
    silu = sb("silu", [P, KT, 2])
    sig = sb("sig", [P, 32])
    start_sum = sb("start_sum", [P, 2 * KT, 2])
    mod_sum = sb("mod_sum", [P, KT])
    tick = sb("tick", [P, 4])
    modc_col = sb("modc_col", [P, 32])
    a_col = sb("a_col", [P, 6, KT])
    rms = sb("rms", [P, 2, T])
    eps_col = sb("eps_col", [P, 2])
    assert base[0] <= nc.sbuf_usable_end, base[0]

    x_rows = place("x_rows", [P, 2, D], F32, shared)
    c_rows = place("c_rows", [P, 2, D], F32, shared + 16384)
    ctxT = place("ctxT", [P, KT, T], F32, shared + 32768)
    vec_rows = place("vec_rows", [P, 3, P], F32, shared + 59392)
    start_rows = place("start_rows", [4, 2 * D], F32, shared)
    silu4 = place("silu4", [P, KT, P], F32R, base_ada_sum)
    sq = place("sq", [P, 2, 2, T], F32, shared + 49152)
    tn = place("tn", [P, 2, 2, T], F32, shared + 53248)
    hc_hi = place("hc_hi", [P, KT, T], F32R, shared)
    hc_lo = place("hc_lo", [P, KT, T], F32R, shared + 16384)
    qT = place("qT", [P, HEADS, T], F32, shared)
    prob = place("prob", [P, 3, 2 * T], F32, shared + 16384)
    probT = place("probT", [P, 2, 4, T], F32, shared + 22528)
    kT = place("kT", [P, KV_HEADS, 2 * T], F32, shared + 32768)
    vS = place("vS", [P, 4, KV_HEADS * HD], F32, shared + 40960)
    hsq = place("hsq", [P, 2, 2 * T], F32, shared + 49152)
    hrms = place("hrms", [P, 2 * T], F32, shared + 53248)
    hrot = place("hrot", [P, 2 * T], F32, shared + 55296)
    rope = place("rope", [P, 2, T], F32, shared + 57344)
    nmax = place("nmax", [P, 32, 4], F32, shared + 60928)
    u = place("u", [P, FT, T], F32, shared)
    z_hi = place("z_hi", [P, 2, 2, 2 * T], F32R, shared)
    z_lo = place("z_lo", [P, 2, 2, 2 * T], F32R, shared + 8192)
    dft = place("dft", [P, 2, 3 * T], F32, shared + 16384)
    dft_hi = place("dft_hi", [P, 2, 3 * T], F32R, shared + 22528)
    dft_lo = place("dft_lo", [P, 2, 3 * T], F32R, shared + 28672)
    yT = place("yT", [P, KT, T], F32, shared)
    y_rows = place("y_rows", [P, 2, D], F32, shared + 16384)

    ps = stack.enter_context(nc.psum_tensor("ps", [P, 8, 512], F32))

    def sem(name):
        return stack.enter_context(nc.semaphore(name))

    raw_in = [sem(f"raw_in{i}") for i in range(RAW)]
    ada_in = [sem(f"ada_in{i}") for i in range(2)]
    small_in = sem("small_in")
    x_in = sem("x_in")
    ctx_rows_in = sem("ctx_rows_in")
    dft_in_sem = sem("dft_in_sem")
    ones_set = sem("ones_set")
    silu4_zero = sem("silu4_zero")
    silu4_ready = sem("silu4_ready")
    start_out = sem("start_out")
    start_T = sem("start_T")
    modT_ready = sem("modT_ready")
    mod_part = sem("mod_part")
    hi_ready = sem("hi_ready")
    lo_ready = sem("lo_ready")
    slice_done = sem("slice_done")
    ada_used = sem("ada_used")
    ada_half = sem("ada_half")
    mod_ready = sem("mod_ready")
    vec_T = sem("vec_T")
    vec_ready = sem("vec_ready")
    sig_ready = sem("sig_ready")
    silu_ready = sem("silu_ready")
    start_mods = sem("start_mods")
    a_ready = sem("a_ready")
    rows_T = sem("rows_T")
    rows_out = sem("rows_out")
    sq_ready = sem("sq_ready")
    sq_used = sem("sq_used")
    rms_ready = sem("rms_ready")
    eps_set = sem("eps_set")
    hrms_ready = sem("hrms_ready")
    t_ready = sem("t_ready")
    mod_done = sem("mod_done")
    hhi_ready = sem("hhi_ready")
    h_ready = sem("h_ready")
    k_out = sem("k_out")
    v_out = sem("v_out")
    q_out = sem("q_out")
    hsq_ready = sem("hsq_ready")
    hss_ready = sem("hss_ready")
    dve_step = sem("dve_step")
    hnorm_ready = sem("hnorm_ready")
    hswap_ready = sem("hswap_ready")
    head_ready = sem("head_ready")
    score_ready = sem("score_ready")
    max_ready = sem("max_ready")
    exp_ready = sem("exp_ready")
    prob_ready = sem("prob_ready")
    probT_ready = sem("probT_ready")
    probT_out = sem("probT_out")
    pv_ready = sem("pv_ready")
    o_hi_ready = sem("o_hi_ready")
    o_ready = sem("o_ready")
    x_added = sem("x_added")
    relu_ready = sem("relu_ready")
    u_ready = sem("u_ready")
    held = sem("held")
    ticked = sem("ticked")
    uhi_ready = sem("uhi_ready")
    ulo_ready = sem("ulo_ready")
    dft_hi_ready = sem("dft_hi_ready")
    dft_ready = sem("dft_ready")
    z_mm = sem("z_mm")
    zhi_ready = sem("zhi_ready")
    z_ready = sem("z_ready")
    y_mm = sem("y_mm")
    yhi_ready = sem("yhi_ready")
    y_ready = sem("y_ready")
    fin_ready = sem("fin_ready")
    fin_T = sem("fin_T")
    fin_out = sem("fin_out")
    out_done = sem("out_done")

    wqkv_v = w_qkv[0].rearrange("(q k p) n -> q p k n", p=P, k=2)
    wo_v = (w_o[0].rearrange("(q k p) n -> q p k n", p=P, k=2),
            fourier_w[0].rearrange("(q k p) n -> q p k n", p=P, k=2))
    w1_v = [w1[l].rearrange("(q k p) (i b n) -> i b q p k n", p=P, k=2, b=2, n=NC) for l in range(2)]
    w2_v = [w2[l].rearrange("(g q k p) n -> g q p k n", p=P, k=2, q=4) for l in range(2)]
    ada_v = [ada_w[l].rearrange("(t p) (m n) -> m t p n", p=P, n=D) for l in range(2)]

    block = stack.enter_context(nc.Block())

    @block.sync
    def _(sp):
        def load_piece(piece, src, it=None, stride=0):
            if it is None:
                if piece >= RAW:
                    sp.wait_ge(lo_ready, 2 * (piece - RAW) + 2)
            else:
                sp.wait_ge(lo_ready, 2 * stride * it + (2 * (piece - RAW) + 2))
            sp.dma_start(raw[:, piece % RAW, :, :], src).then_inc(raw_in[piece % RAW], 16)

        for n in range(START):
            load_piece(n, ada_v[0][n // KT, n % KT].rearrange("p (k n) -> p k n", k=2))
        for q in range(8):
            load_piece(P_KV + q, wqkv_v[q, :, :, D:D + NC])
        for b in range(2):
            for q in range(8):
                load_piece(P_Q + 8 * b + q, wqkv_v[q, :, :, b * NC:(b + 1) * NC])
        for l in range(2):
            for b in range(2):
                for q in range(8):
                    load_piece(P_WO[l] + 8 * b + q, wo_v[l][q, :, :, b * NC:(b + 1) * NC])
            with sp.Fori(0, 4) as it:
                for b in range(2):
                    for q in range(8):
                        load_piece(P_UP[l] + 8 * b + q, w1_v[l][it, b, q], it, 16)
            for s in range(2):
                with sp.Fori(0, 8) as g:
                    for i in range(4):
                        load_piece(P_DOWN[l] + 32 * s + i, w2_v[l][g, i, :, :, s * NC:(s + 1) * NC], g, 4)
        sp.wait_ge(out_done, 32)

    @block.gpsimd
    def _(pool):
        def load_ada(n, src):
            if n >= 2:
                pool.wait_ge(ada_used, n - 1)
            pool.dma_start(ada_raw[:, n % 2, :], src).then_inc(ada_in[n % 2], 16)

        def load_ada_in_loop(n, dst, src, it, stride, ticks):
            pool.wait_ge(ticked, it * stride + ticks)
            pool.wait_ge(ada_used, it * stride + (n - 1))
            nc.gpsimd.tensor_tensor(tick[:, 0:1], tick[:, 1:2], tick[:, 1:2], ALU.add).then_inc(ticked, 1)
            pool.dma_start(dst, src).then_inc(ada_in[n % 2], 16)

        def load_vector(i):
            lay, m = SUMS[i]
            for t in range(KT):
                load_ada(16 * i + t, ada_v[lay][m, t])

        def load_in_sweep(i, ticks):
            lay, m = SUMS[i]
            src = ada_w[lay, :, m * D:(m + 1) * D].rearrange("(g a p) n -> g a p n", a=2, p=P)
            with pool.Fori(0, 8) as g:
                for a in range(2):
                    load_ada_in_loop(16 * i + a, ada_raw[:, a, :], src[g, a], g, 2, ticks + a)

        nc.gpsimd.memset(tick[:, 0:2], 0.0).then_inc(ticked, 1)
        for i in range(HALVES):
            load_vector(i)
        halves = ada_w[1, :, D:3 * D].rearrange("(i k p) (h n) -> h i p k n", p=P, k=2, n=NC)
        with pool.Fori(0, 4) as it:
            for i in range(8):
                load_ada_in_loop(16 * HALVES + i, ada_raw[:, i % 2, :].rearrange("p (k n) -> p k n", k=2), halves[it, i],
                                 it, 8, i + 1)
        load_in_sweep(6, 33)
        load_in_sweep(7, 49)
        load_vector(8)
        load_in_sweep(9, 65)

    @block.scalar
    def _(act):
        def split_hi(s, it=None, stride=0):
            piece = s // 2
            if it is None:
                act.wait_ge(raw_in[piece % RAW], 16 * (piece // RAW + 1))
                if s >= SPLIT:
                    act.wait_ge(slice_done, s - SPLIT + 1)
            else:
                act.wait_ge(raw_in[piece % RAW], it * (stride // 2 // RAW * 16) + 16 * (piece // RAW + 1))
                act.wait_ge(slice_done, it * stride + (s - SPLIT + 1))
            act.activation(w_hi[:, s % SPLIT, :], raw[:, piece % RAW, s % 2, :], ACT.Copy).then_inc(hi_ready, 1)

        def hold(wait_sem, value, held_before):
            act.wait_ge(held, held_before)
            act.wait_ge(wait_sem, value)
            act.activation(sig[:, 0:1], sig[:, 1:2], ACT.Copy).then_inc(held, 1)

        def split_block(first, hook=None, it=None, stride=0, pieces=8):
            for p in range(pieces):
                if hook:
                    hook(p)
                for s in (first + 2 * p + LOOKAHEAD, first + 2 * p + 1 + LOOKAHEAD):
                    if it is not None or s < LAST_SLICE:
                        split_hi(s, it, stride)

        def square_pair(n, i, src):
            if 8 * n + i >= 2:
                act.wait_ge(sq_used, 8 * n + i - 1)
            act.activation(sq[:, i % 2], src[:, 2 * i:2 * i + 2, :], ACT.Square).then_inc(sq_ready, 1)

        def squares(n, added, pairs):
            for i in pairs:
                act.wait_ge(x_added, added if i < 4 else added + 2 * (i - 3))
                square_pair(n, i, xT)

        def root(n, bank, slot):
            act.wait_ge(sq_used, 8 * n + 8)
            if n >= 2:
                act.wait_ge(t_ready, 8 * n)
            act.activation(rms[:, slot, :], ps[:, bank, 0:T], ACT.Sqrt, bias=eps_col[:, 0:1]).then_inc(rms_ready, 1)

        def modulate(n, i, shift, dst):
            act.wait_ge(t_ready, 8 * n + i + 1)
            for k in range(2):
                kt = 2 * i + k
                act.activation(tn[:, i % 2, k], tn[:, i % 2, k], ACT.Identity, bias=shift[:, kt:kt + 1],
                               scale=a_col[:, n, kt:kt + 1]).then_inc(mod_done, 1)
            act.wait_ge(mod_done, 2 * (8 * n + i + 1))
            act.activation(dst[:, 2 * i:2 * i + 2, :], tn[:, i % 2], ACT.Copy).then_inc(hhi_ready, 1)

        act.wait_ge(ticked, 1)
        act.activation(tick[:, 2:3], tick[:, 1:2], ACT.Copy).then_inc(held, 1)
        act.activation(tick[:, 3:4], tick[:, 1:2], ACT.Copy).then_inc(u_ready, 1)
        act.dma_start(vec_rows[0:96, 0, :], ada_b[0].rearrange("(t p) -> t p", p=P)).then_inc(small_in, 16)
        act.dma_start(vec_rows[0:96, 1, :], ada_b[1].rearrange("(t p) -> t p", p=P)).then_inc(small_in, 16)
        for r, n, v in ((V_C, 16, c[0]), (V_CC, 16, c_ctx), (V_FIN, 16, final_g), (V_QG, 1, q_g[0]), (V_KG, 1, k_g[0])):
            act.dma_start(vec_rows[r:r + n, 2, :], v.rearrange("(t p) -> t p", p=P)).then_inc(small_in, 16)
        act.dma_start(vec_rows[V_MIX:V_MIX + 32, 2, :], norm_mix_g.rearrange("l (t p) -> (l t) p", p=P)).then_inc(small_in, 16)
        act.dma_start(vec_rows[V_MLP:V_MLP + 32, 2, :], norm_mlp_g.rearrange("l (t p) -> (l t) p", p=P)).then_inc(small_in, 16)
        act.dma_start(ident[:, :], ident_in).then_inc(small_in, 16)
        act.dma_start(swap[:, :], swap_in).then_inc(small_in, 16)
        act.dma_start(rope[:, :, :], rope_in.rearrange("a p t -> p a t")).then_inc(small_in, 16)
        act.dma_start(x_rows[:, :, :], x[0].rearrange("(a p) d -> p a d", p=P)).then_inc(x_in, 16)
        act.dma_start(c_rows[:, :, :], ctx_in[0].rearrange("(a p) d -> p a d", p=P)).then_inc(ctx_rows_in, 16)
        act.wait_ge(vec_ready, 3)
        act.activation(sig[:, :], misc[:, 0:32], ACT.Sigmoid).then_inc(sig_ready, 1)
        act.wait_ge(eps_set, 2)
        act.wait_ge(silu_ready, 1)
        act.wait_ge(silu4_zero, 1)
        act.activation(silu4[:, :, 0:4:2], silu[:, :, :], ACT.Copy).then_inc(silu4_ready, 1)

        def start_rows_out(m):
            act.wait_ge(slice_done, 32 * (m + 1))
            act.activation(start_rows[:, m * D:(m + 1) * D], ps[0:4, 4:8, :].rearrange("p b n -> p (b n)"),
                           ACT.Copy).then_inc(start_out, 1)

        def start_hook(n):
            if n == 16:
                act.wait_ge(rows_T, 16)
                start_rows_out(0)
            if n >= 16:
                st = (n - 16) // 8
                if n % 8 == 0:
                    act.wait_ge(rows_out, 8 * st + 8)
                square_pair(st, n % 8, (xT, ctxT)[st])

        for s in range(LOOKAHEAD):
            split_hi(s)
        split_block(0, start_hook, pieces=START)
        start_rows_out(1)
        root(0, 2, 0)
        root(1, 3, 1)

        def both(i):
            for n, dst, shift in ((0, h_hi, mod_col), (1, hc_hi, modc_col)):
                c0 = 2 * i + n
                act.wait_ge(t_ready, c0 + 1)
                for k in range(2):
                    kt = 2 * i + k
                    act.activation(tn[:, n, k], tn[:, n, k], ACT.Identity, bias=shift[:, kt:kt + 1],
                                   scale=a_col[:, n, kt:kt + 1]).then_inc(mod_done, 1)
                act.wait_ge(mod_done, 2 * (c0 + 1))
                act.activation(dst[:, 2 * i:2 * i + 2, :], tn[:, n], ACT.Copy).then_inc(hhi_ready, 1)

        act.wait_ge(a_ready, 2)
        both(0)
        split_block(2 * P_KV, lambda p: both(p + 1) if p < 7 else None)
        act.wait_ge(slice_done, 2 * P_Q)
        for g in range(KV_HEADS):
            act.activation(kT[:, g, :], ps[:, g, :], ACT.Copy).then_inc(k_out, 1)

        def head_src(r):
            return kT[:, r, :] if r < 4 else qT[:, 2 * (r - 4):2 * (r - 4) + 2, :].rearrange("p a t -> p (a t)")

        def head_square(r):
            if r < 4:
                act.wait_ge(k_out, 4)
            else:
                act.wait_ge(q_out, 4 if r < 8 else 8)
            if r >= 2:
                act.wait_ge(hss_ready, r - 1)
            act.activation(hsq[:, r % 2, :], head_src(r), ACT.Square).then_inc(hsq_ready, 1)

        def head_root(r, bank):
            act.wait_ge(hss_ready, r + 1)
            if r:
                act.wait_ge(hnorm_ready, r)
            act.activation(hrms[:, :], ps[:, bank, :], ACT.Sqrt, bias=eps_col[:, 1:2]).then_inc(hrms_ready, 1)

        def head_hook(r0, bank):
            return lambda p: head_square(r0 + p // 2) if p % 2 == 0 else head_root(r0 + p // 2, bank)

        split_block(2 * P_Q, head_hook(0, 5))
        for b in range(2):
            act.wait_ge(slice_done, 2 * P_Q + 16 * (b + 1))
            for i in range(4):
                act.activation(qT[:, 8 * b + 2 * i:8 * b + 2 * i + 2, :].rearrange("p a t -> p (a t)"),
                               ps[:, 4 * b + i, :], ACT.Copy).then_inc(q_out, 1)
            if b == 0:
                split_block(2 * P_Q + 16, head_hook(4, 1))

        for n in range(37):
            if n < 32:
                act.wait_ge(max_ready, n + 1)
                if n >= 3:
                    act.wait_ge(probT_ready, n - 2)
                act.activation(prob[:, n % 3, :], ps[:, n % 3, :], ACT.Exp, bias=nmax[:, n, 1:2], scale=SCALE,
                               accum_out=nmax[:, n, 2:3]).then_inc(exp_ready, 1)
            if n % 3 == 1 and n <= 10:
                head_square(8 + n // 3)
            if n % 3 == 2 and n <= 11:
                head_root(8 + n // 3, 7)
            m = n - 2
            if 0 <= m < 32:
                h, qt = m // 2, m % 2
                act.wait_ge(probT_ready, m + 1)
                if h >= 2:
                    act.wait_ge(pv_ready, h - 1)
                act.activation(probT[:, h % 2, :, qt * P:(qt + 1) * P],
                               ps[:, 3 + m % 2, :].rearrange("p (s q) -> p s q", s=4), ACT.Copy).then_inc(probT_out, 1)
            if n >= 5 and n % 2 == 1:
                h = (n - 5) // 2
                act.wait_ge(pv_ready, h + 1)
                act.activation(h_hi[:, h, :], ps[:, 5 + h % 2, 0:T], ACT.Copy).then_inc(o_hi_ready, 1)

        for l in range(2):
            n = 2 + 2 * l
            if l == 1:
                squares(3, 24, range(2))
                act.wait_ge(slice_done, 2 * P_WO[1])
                act.wait_ge(ulo_ready, 64)
                act.dma_start(dft[:, :, :], dft_in.rearrange("(k p) n -> p k n", p=P)).then_inc(dft_in_sem, 16)
                squares(3, 24, range(2, 8))
                root(3, 0, 0)
                act.wait_ge(dft_in_sem, 16)
                act.activation(dft_hi[:, :, :], dft[:, :, :], ACT.Copy).then_inc(dft_hi_ready, 1)
                act.wait_ge(a_ready, 4)
                for i in range(2):
                    modulate(3, i, mod_col[:, 96:112], h_hi)
                for g in range(9):
                    if g < 8:
                        for nt in range(2):
                            act.wait_ge(z_mm, 2 * g + nt + 1)
                            if g >= 2:
                                act.wait_ge(y_mm, g - 1)
                            act.activation(z_hi[:, g % 2, nt, :], ps[:, 2 * (g % 2) + nt, :], ACT.Copy).then_inc(zhi_ready, 1)
                    if g + 2 < 8:
                        modulate(3, g + 2, mod_col[:, 96:112], h_hi)
                    if g >= 1:
                        act.wait_ge(y_mm, g)
                        act.activation(h_hi[:, 2 * g - 2:2 * g, :].rearrange("p a t -> p (a t)"), ps[:, 4 + (g - 1) % 2, :],
                                       ACT.Copy, scale=1.0 / T).then_inc(yhi_ready, 1)
            split_block(2 * P_WO[l])
            split_block(2 * P_WO[l] + 16)
            squares(n, 8 + 32 * l, range(8))
            root(n, 4, 0)
            act.wait_ge(a_ready, n + 1)
            shift = mod_col[:, 96 * l + 48:96 * l + 64]
            modulate(n, 0, shift, h_hi)

            def relu_square(blk, it=None):
                b = blk % 2
                count = 32 * l + 4 * blk
                if it is None:
                    act.wait_ge(slice_done, 2 * P_UP[l] + 16 * (blk + 1))
                    f0 = 8 * blk
                    rows = u[:, f0:f0 + 8, :]
                else:
                    hold(slice_done, it * 32 + (2 * P_UP[l] + 16 * (blk + 1)), it * 4 + (12 * l - 3 + 2 * b))
                    rows = u[:, bass.ds(it * 16 + 8 * blk, 8), :]
                for j in range(4):
                    act.activation(rows[:, 2 * j:2 * j + 2, :], ps[:, 4 * b + j, :].rearrange("p (a t) -> p a t", a=2),
                                   ACT.Relu).then_inc(relu_ready, 1)
                if it is None:
                    act.wait_ge(relu_ready, count + 4)
                else:
                    hold(relu_ready, it * 8 + (count + 4), it * 4 + (12 * l - 3 + 2 * b + 1))
                act.activation(rows, rows, ACT.Square).then_inc(u_ready, 1)

            split_block(2 * P_UP[l], lambda p: modulate(n, p + 1, shift, h_hi) if p < 7 else None)
            relu_square(0)
            split_block(2 * P_UP[l] + 16)
            relu_square(1)
            with act.Fori(1, 4) as it:
                for b in range(2):
                    split_block(2 * P_UP[l] + 16 * b, None, it, 32)
                    relu_square(b, it)

            def u_hi(s, i, g=None):
                slot = i % 4
                if g is None:
                    src = u[:, 2 * i:2 * i + 2, :]
                else:
                    src = u[:, bass.ds(g * 8 + 2 * i, 2), :]
                act.activation(h_hi[:, 2 * slot:2 * slot + 2, :], src, ACT.Copy).then_inc(uhi_ready, 1)

            for s in range(2):
                first = 2 * P_DOWN[l] + 64 * s
                if s == 0:
                    act.wait_ge(slice_done, first)
                    act.wait_ge(u_ready, 8 * (l + 1) + 1)
                    u_hi(0, 0)
                for p in range(4):
                    u_hi(s, p + 1)
                    for q in (0, 1):
                        split_hi(first + 2 * p + q + LOOKAHEAD)
                with act.Fori(1, 7) as g:
                    for p in range(4):
                        u_hi(s, p + 1, g)
                        for q in (0, 1):
                            split_hi(first + 2 * p + q + LOOKAHEAD, g, 8)
                for p in range(28, 32):
                    if p < 31:
                        u_hi(s, p + 1)
                    elif s == 0:
                        u_hi(1, 0)
                    for q in (0, 1):
                        if first + 2 * p + q + LOOKAHEAD < LAST_SLICE:
                            split_hi(first + 2 * p + q + LOOKAHEAD)
        squares(5, 56, range(8))
        root(5, 0, 0)
        for i in range(8):
            act.wait_ge(t_ready, 40 + i + 1)
            for k in range(2):
                act.activation(yT[:, 2 * i + k, :], tn[:, i % 2, k], ACT.Copy,
                               scale=a_col[:, 5, 2 * i + k:2 * i + k + 1]).then_inc(fin_ready, 1)
        for tt in range(2):
            act.wait_ge(fin_out, 4 * tt + 4)
            act.dma_start(out[0, tt * P:(tt + 1) * P, :], y_rows[:, tt, :]).then_inc(out_done, 16)

    @block.vector
    def _(dve):
        def split_lo(s, it=None, stride=0):
            if it is None:
                dve.wait_ge(hi_ready, s + 1)
            else:
                dve.wait_ge(hi_ready, it * stride + (s + 1))
            nc.vector.tensor_tensor(w_lo[:, s % SPLIT, :], raw[:, s // 2 % RAW, s % 2, :],
                                    w_hi[:, s % SPLIT, :].bitcast(F32), ALU.subtract).then_inc(lo_ready, 1)

        def ada_step(n, first, t, it=None, stride=0):
            if it is None:
                dve.wait_ge(ada_in[n % 2], 16 * (n // 2 + 1))
                if n > 0:
                    dve.wait_ge(ada_used, n)
            else:
                dve.wait_ge(ada_in[n % 2], it * (8 * stride) + 16 * (n // 2 + 1))
                dve.wait_ge(ada_used, it * stride + n)
            if isinstance(t, int):
                col = silu[:, t, 0:1]
            else:
                col = silu[:, bass.ds(t, 1), 0:1].rearrange("p a b -> p (a b)")
            if first:
                ins = nc.vector.tensor_scalar(ada_sum[:, :], ada_raw[:, n % 2, :], col, None, ALU.mult)
            else:
                ins = nc.vector.scalar_tensor_tensor(ada_sum[:, :], ada_raw[:, n % 2, :], col, ada_sum[:, :],
                                                     ALU.mult, ALU.add)
            ins.then_inc(ada_used, 1)

        def ada_half_step(i, it=None):
            n = 16 * HALVES + i
            if it is None:
                dve.wait_ge(ada_in[n % 2], 16 * (n // 2 + 1))
                dve.wait_ge(ada_used, n)
            else:
                dve.wait_ge(ada_in[n % 2], it * 64 + 16 * (n // 2 + 1))
                dve.wait_ge(ada_used, it * 8 + n)
            acc = ada_sum[:, 0:NC]
            if i == 0:
                ins = nc.vector.tensor_scalar(acc, ada_raw[:, n % 2, 0:NC], silu[:, 0, 0:1], None, ALU.mult)
            else:
                ins = nc.vector.scalar_tensor_tensor(acc, ada_raw[:, n % 2, 0:NC], silu[:, 2 * i, 0:1], acc, ALU.mult, ALU.add)
            ins.then_inc(ada_half, 1)
            if it is None:
                dve.wait_ge(ada_half, i + 1)
            else:
                dve.wait_ge(ada_half, it * 8 + (i + 1))
            nc.vector.scalar_tensor_tensor(acc, ada_raw[:, n % 2, NC:2 * NC], silu[:, 2 * i + 1, 0:1], acc, ALU.mult,
                                           ALU.add).then_inc(ada_used, 1)

        def take_half(it=None):
            col = 96 + KT
            for b in range(2):
                if it is None:
                    dve.wait_ge(modT_ready, 4 * HALVES + b + 1)
                else:
                    dve.wait_ge(modT_ready, it * 2 + (4 * HALVES + b + 1))
                nc.vector.tensor_reduce(mod_sum[:, 4 * b:4 * b + 4], ps[:, b, :].rearrange("p (f k) -> p f k", f=4),
                                        AX_X, ALU.add).then_inc(mod_part, 1)
            if it is None:
                dve.wait_ge(mod_part, 4 * HALVES + 2)
                dst, bias = mod_col[:, col:col + 8], bias_col[:, col:col + 8]
            else:
                dve.wait_ge(mod_part, it * 2 + (4 * HALVES + 2))
                dst, bias = mod_col[:, bass.ds(it * 8 + col, 8)], bias_col[:, bass.ds(it * 8 + col, 8)]
            nc.vector.tensor_tensor(dst, mod_sum[:, 0:8], bias, ALU.add).then_inc(mod_ready, 1)

        def take_mod(i, bank0, col, it=None):
            for b in range(4):
                if it is None:
                    dve.wait_ge(modT_ready, 4 * i + b + 1)
                else:
                    dve.wait_ge(modT_ready, it * 4 + (4 * i + b + 1))
                nc.vector.tensor_reduce(mod_sum[:, 4 * b:4 * b + 4], ps[:, bank0 + b, :].rearrange("p (f k) -> p f k", f=4),
                                        AX_X, ALU.add).then_inc(mod_part, 1)
            if it is None:
                dve.wait_ge(mod_part, 4 * i + 4)
                dst, bias = mod_col[:, col:col + 16], bias_col[:, col:col + 16]
            else:
                dve.wait_ge(mod_part, it * 4 + (4 * i + 4))
                dst, bias = mod_col[:, bass.ds(it * 16 + col, 16)], bias_col[:, bass.ds(it * 16 + col, 16)]
            nc.vector.tensor_tensor(dst, mod_sum[:, :], bias, ALU.add).then_inc(mod_ready, 1)

        def gain(n, g0, scale_cols, wait):
            dve.wait_ge(*wait)
            nc.vector.scalar_tensor_tensor(a_col[:, n, :], scale_cols, 1.0, misc[:, g0:g0 + KT], ALU.add,
                                           ALU.mult).then_inc(dve_step, 1)
            steps[0] += 1
            dve.wait_ge(dve_step, steps[0])
            nc.vector.tensor_scalar(a_col[:, n, :], a_col[:, n, :], ROOT_D, None, ALU.mult).then_inc(a_ready, 1)

        steps = [0]
        lowered = {}

        def step(ins):
            ins.then_inc(dve_step, 1)
            steps[0] += 1
            dve.wait_ge(dve_step, steps[0])

        def invert_rms(n, slot):
            dve.wait_ge(rms_ready, n + 1)
            step(nc.vector.reciprocal(rms[:, slot, :], rms[:, slot, :]))

        def normalise(i, src, slot, r):
            if slot in lowered:
                dve.wait_ge(h_ready, lowered[slot])
            nc.vector.tensor_tensor(tn[:, slot], src[:, 2 * i:2 * i + 2, :],
                                    rms[:, r:r + 1, :].to_broadcast([P, 2, T]), ALU.mult).then_inc(t_ready, 1)

        def lower(c0, i, slot, hi, lo):
            lowered[slot] = c0 + 1
            dve.wait_ge(hhi_ready, c0 + 1)
            nc.vector.tensor_tensor(lo[:, 2 * i:2 * i + 2, :], tn[:, slot],
                                    hi[:, 2 * i:2 * i + 2, :].bitcast(F32), ALU.subtract).then_inc(h_ready, 1)

        def split_block(first, hook=None, ada=None, it=None, stride=0, pieces=8):
            for p in range(pieces):
                if hook:
                    hook(p)
                if ada:
                    ada(p)
                for s in (first + 2 * p + LOOKAHEAD, first + 2 * p + 1 + LOOKAHEAD):
                    split_lo(s, it, stride)

        def add_gated(l, m, wait, bank0, tiles):
            dve.wait_ge(*wait)
            for j in range(8):
                kt = tiles + j
                ins = nc.vector.scalar_tensor_tensor(xT[:, kt, :], ps[:, bank0 + j // 2, (j % 2) * T:(j % 2 + 1) * T],
                                                     mod_col[:, 96 * l + 16 * m + kt:96 * l + 16 * m + kt + 1],
                                                     xT[:, kt, :], ALU.mult, ALU.add)
                ins.then_inc(x_added, 1)

        nc.vector.memset(silu4[:, :, :].bitcast(F32), 0.0).then_inc(silu4_zero, 1)
        nc.vector.memset(ones[:, :], 1.0).then_inc(ones_set, 1)
        nc.vector.memset(eps_col[:, 0:1], EPS * D).then_inc(eps_set, 1)
        nc.vector.memset(eps_col[:, 1:2], EPS * HD).then_inc(eps_set, 1)
        for i, (dst, w) in enumerate(((bias_col[:, 0:96], 96), (bias_col[:, 96:192], 96), (misc[:, :], N_MISC))):
            dve.wait_ge(vec_T, 3)
            nc.vector.tensor_copy(dst, ps[:, 0, i * P:i * P + w]).then_inc(vec_ready, 1)
        dve.wait_ge(sig_ready, 1)
        nc.vector.tensor_tensor(silu[:, :, :], misc[:, 0:32].rearrange("p (a t) -> p t a", a=2),
                                sig[:, :].rearrange("p (a t) -> p t a", a=2), ALU.mult).then_inc(silu_ready, 1)
        dve.wait_ge(silu4_ready, 1)
        nc.vector.tensor_tensor(silu4[:, :, 1:4:2], silu[:, :, :], silu4[:, :, 0:4:2].bitcast(F32),
                                ALU.subtract).then_inc(silu4_ready, 1)

        def start_hook(n):
            if 2 <= n < 18:
                v = n - 2
                dst = (xT if v < 8 else ctxT)[:, 2 * (v % 8):2 * (v % 8) + 2, :].rearrange("p a t -> p (a t)")
                dve.wait_ge(rows_T, v + 1)
                nc.vector.tensor_copy(dst, ps[:, v % 2, :]).then_inc(rows_out, 1)

        for s in range(LOOKAHEAD):
            split_lo(s)
        split_block(0, start_hook, pieces=START)
        invert_rms(0, 0)
        invert_rms(1, 1)
        dve.wait_ge(start_T, 1)
        step(nc.vector.tensor_reduce(start_sum[:, :, :].rearrange("p f a -> p (f a)"),
                                     ps[:, 0, 0:P].rearrange("p (f h) -> p f h", h=2), AX_X, ALU.add))
        nc.vector.tensor_tensor(mod_col[:, 0:32], start_sum[:, :, 0], bias_col[:, 0:32], ALU.add).then_inc(start_mods, 1)
        nc.vector.tensor_tensor(modc_col[:, :], start_sum[:, :, 1], bias_col[:, 0:32], ALU.add).then_inc(start_mods, 1)
        gain(0, V_MIX, mod_col[:, 16:32], (start_mods, 2))
        gain(1, V_MIX, modc_col[:, 16:32], (start_mods, 2))

        def norm_both(i):
            for n, src in ((0, xT), (1, ctxT)):
                normalise(i, src, n, n)

        def lower_both(i):
            for n, hi, lo in ((0, h_hi, h_lo), (1, hc_hi, hc_lo)):
                lower(2 * i + n, i, n, hi, lo)

        norm_both(0)
        lower_both(0)

        def kv_hook(p):
            if p < 7:
                norm_both(p + 1)
                lower_both(p + 1)

        def kv_ada(p):
            for t in (2 * p, 2 * p + 1):
                ada_step(t, t == 0, t)

        split_block(2 * P_KV, kv_hook, kv_ada)
        dve.wait_ge(slice_done, 2 * P_Q)
        for st in range(4):
            nc.vector.tensor_copy(vS[:, st, :], ps[:, 4 + st, :]).then_inc(v_out, 1)
        take_mod(0, 4, 32)
        step(nc.vector.tensor_scalar(misc[:, V_QG:V_KG + 1], misc[:, V_QG:V_KG + 1], ROOT_HD, None, ALU.mult))

        def head_src(r):
            return kT[:, r, :] if r < 4 else qT[:, 2 * (r - 4):2 * (r - 4) + 2, :].rearrange("p a t -> p (a t)")

        def head_norm(r):
            dve.wait_ge(hrms_ready, r + 1)
            step(nc.vector.reciprocal(hrms[:, :], hrms[:, :]))
            g = V_KG if r < 4 else V_QG
            nc.vector.scalar_tensor_tensor(head_src(r), head_src(r), misc[:, g:g + 1], hrms[:, :], ALU.mult,
                                           ALU.mult).then_inc(hnorm_ready, 1)

        def head_rope(r, bank):
            heads = 1 if r < 4 else 2
            dve.wait_ge(hswap_ready, r + 1)
            dst = head_src(r)[:, 0:heads * T].rearrange("p (a t) -> p a t", a=heads)
            sw = ps[:, bank, 0:heads * T].rearrange("p (a t) -> p a t", a=heads)
            rot = hrot[:, 0:heads * T].rearrange("p (a t) -> p a t", a=heads)
            cos = rope[:, 0:1, :].to_broadcast([P, heads, T])
            sin = rope[:, 1:2, :].to_broadcast([P, heads, T])
            if r:
                dve.wait_ge(head_ready, r)
            step(nc.vector.tensor_tensor(rot, sw, sin, ALU.mult))
            step(nc.vector.tensor_tensor(dst, dst, cos, ALU.mult))
            nc.vector.tensor_tensor(dst, dst, rot, ALU.add).then_inc(head_ready, 1)

        def head_hook(r0, bank):
            def hook(p):
                if p % 2 == 1:
                    if p > 1:
                        head_rope(r0 + p // 2 - 1, bank + 1)
                    head_norm(r0 + p // 2)
            return hook

        for b in range(2):
            split_block(2 * P_Q + 16 * b, head_hook(4 * b, 5 if b == 0 else 1),
                        lambda p: ada_step(16 + 8 * b + p, b == 0 and p == 0, 8 * b + p))
            head_rope(4 * b + 3, 6 if b == 0 else 2)
        take_mod(1, 0, 48)

        for n in range(37):
            if n < 32 and n % 2 == 0:
                ada_step(32 + n // 2, n == 0, n // 2)
            if n < 32:
                dve.wait_ge(score_ready, n + 1)
                step(nc.vector.tensor_reduce(nmax[:, n, 0:1], ps[:, n % 3, :], AX_X, ALU.max))
                nc.vector.tensor_scalar(nmax[:, n, 1:2], nmax[:, n, 0:1], -SCALE, None, ALU.mult).then_inc(max_ready, 1)
            m = n - 1
            if 0 <= m < 32:
                dve.wait_ge(exp_ready, m + 1)
                step(nc.vector.reciprocal(nmax[:, m, 3:4], nmax[:, m, 2:3]))
                nc.vector.tensor_scalar(prob[:, m % 3, :], prob[:, m % 3, :], nmax[:, m, 3:4], None,
                                        ALU.mult).then_inc(prob_ready, 1)
            if n % 3 == 2 and n <= 11:
                head_norm(8 + n // 3)
            if n % 3 == 1 and 4 <= n <= 13:
                head_rope(8 + n // 3 - 1, 7)
            if n >= 5 and n % 2 == 1:
                h = (n - 5) // 2
                dve.wait_ge(o_hi_ready, h + 1)
                nc.vector.tensor_tensor(h_lo[:, h, :], ps[:, 5 + h % 2, 0:T], h_hi[:, h, :].bitcast(F32),
                                        ALU.subtract).then_inc(o_ready, 1)

        take_mod(2, 0, 64)
        for l in range(2):
            n = 2 + 2 * l
            if l == 1:
                gain(3, V_MIX + KT, mod_col[:, 96 + 16:96 + 32], (mod_ready, mods_ready(7)))
                invert_rms(3, 0)
                dve.wait_ge(dft_hi_ready, 1)
                nc.vector.tensor_tensor(dft_lo[:, :, :], dft[:, :, :], dft_hi[:, :, :].bitcast(F32),
                                        ALU.subtract).then_inc(dft_ready, 1)
                normalise(0, xT, 0, 0)
                normalise(1, xT, 1, 0)
                for i in range(2):
                    lower(24 + i, i, i % 2, h_hi, h_lo)
                    normalise(i + 2, xT, i % 2, 0)
                for g in range(9):
                    if g < 8:
                        for nt in range(2):
                            dve.wait_ge(zhi_ready, 2 * g + nt + 1)
                            nc.vector.tensor_tensor(z_lo[:, g % 2, nt, :], ps[:, 2 * (g % 2) + nt, :],
                                                    z_hi[:, g % 2, nt, :].bitcast(F32), ALU.subtract).then_inc(z_ready, 1)
                    if g + 2 < 8:
                        lower(24 + g + 2, g + 2, g % 2, h_hi, h_lo)
                        if g + 4 < 8:
                            normalise(g + 4, xT, g % 2, 0)
                    if g >= 1:
                        dve.wait_ge(yhi_ready, g)
                        nc.vector.scalar_tensor_tensor(h_lo[:, 2 * g - 2:2 * g, :].rearrange("p a t -> p (a t)"),
                                                       ps[:, 4 + (g - 1) % 2, :], 1.0 / T,
                                                       h_hi[:, 2 * g - 2:2 * g, :].rearrange("p a t -> p (a t)").bitcast(F32),
                                                       ALU.mult, ALU.subtract).then_inc(y_ready, 1)
            s = 3 if l == 0 else 8
            for b in range(2):
                split_block(2 * P_WO[l] + 16 * b, None,
                            lambda p: ada_step(16 * s + 8 * b + p, b == 0 and p == 0, 8 * b + p))
                add_gated(l, 2, (slice_done, 2 * P_WO[l] + 16 * (b + 1)), 4 * b, 8 * b)
            lay, m = SUMS[s]
            take_mod(s, 0, 96 * lay + 16 * m)
            gain(n, V_MLP + KT * l, mod_col[:, 96 * l + 64:96 * l + 80], (mod_ready, mods_ready(s)))
            invert_rms(n, 0)
            normalise(0, xT, 0, 0)
            normalise(1, xT, 1, 0)
            lower(8 * n, 0, 0, h_hi, h_lo)

            def feed(p):
                if p < 6:
                    normalise(p + 2, xT, p % 2, 0)
                if p < 7:
                    lower(8 * n + p + 1, p + 1, (p + 1) % 2, h_hi, h_lo)

            for b in range(2):
                split_block(2 * P_UP[l] + 16 * b, feed if b == 0 else None,
                            (lambda p: ada_half_step(4 * b + p // 2) if p % 2 == 0 else None) if l == 0 else None)
            if l == 0:
                take_half()
            with dve.Fori(1, 4) as it:
                for b in range(2):
                    split_block(2 * P_UP[l] + 16 * b, None,
                                (lambda p: ada_half_step(4 * b + p // 2, it) if p % 2 == 0 else None) if l == 0 else None,
                                it, 32)
                if l == 0:
                    take_half(it)

            def u_lo(s, i, g=None):
                slot = i % 4
                if g is None:
                    dve.wait_ge(uhi_ready, 64 * l + 32 * s + i + 1)
                    src = u[:, 2 * i:2 * i + 2, :]
                else:
                    dve.wait_ge(uhi_ready, g * 4 + (64 * l + 32 * s + i + 1))
                    src = u[:, bass.ds(g * 8 + 2 * i, 2), :]
                nc.vector.tensor_tensor(h_lo[:, 2 * slot:2 * slot + 2, :], src,
                                        h_hi[:, 2 * slot:2 * slot + 2, :].bitcast(F32), ALU.subtract).then_inc(ulo_ready, 1)

            for s in range(2):
                first = 2 * P_DOWN[l] + 64 * s
                vec = {(0, 0): 6, (0, 1): 7, (1, 0): 9}.get((l, s))
                n0 = 16 * vec if vec else None
                if s == 0:
                    u_lo(0, 0)
                for p in range(4):
                    u_lo(s, p + 1)
                    if vec and p % 2 == 0:
                        ada_step(n0 + p // 2, p == 0, p // 2)
                    for q in (0, 1):
                        split_lo(first + 2 * p + q + LOOKAHEAD)
                with dve.Fori(1, 7) as g:
                    for p in range(4):
                        u_lo(s, p + 1, g)
                        if vec and p % 2 == 0:
                            ada_step(n0 + p // 2, False, g * 2 + p // 2, g, 2)
                        for q in (0, 1):
                            split_lo(first + 2 * p + q + LOOKAHEAD, g, 8)
                for p in range(28, 32):
                    if p < 31:
                        u_lo(s, p + 1)
                    elif s == 0:
                        u_lo(1, 0)
                    if vec and p % 2 == 0:
                        ada_step(n0 + p // 2, False, p // 2)
                    for q in (0, 1):
                        if first + 2 * p + q + LOOKAHEAD < LAST_SLICE:
                            split_lo(first + 2 * p + q + LOOKAHEAD)
                if vec:
                    lay, m = SUMS[vec]
                    take_mod(vec, 4 if s == 0 else 0, 96 * lay + 16 * m)
                    dve.wait_ge(mod_ready, mods_ready(vec))
                add_gated(l, 5, (slice_done, first + 64), 4 * s, 8 * s)
        nc.vector.tensor_scalar(a_col[:, 5, :], misc[:, V_FIN:V_FIN + KT], ROOT_D, None, ALU.mult)
        invert_rms(5, 0)
        for i in range(8):
            if i >= 2:
                dve.wait_ge(fin_ready, 2 * (i - 1))
            normalise(i, xT, i % 2, 0)
        for tt in range(2):
            for i in range(4):
                dve.wait_ge(fin_T, 4 * tt + i + 1)
                nc.vector.tensor_copy(y_rows[:, tt, 512 * i:512 * (i + 1)], ps[:, 1 + (4 * tt + i) % 4, :]).then_inc(fin_out, 1)

    @block.tensor
    def _(pe):
        mm = nc.tensor.matmul

        def three(dst, w_h, w_l, m_h, m_l, start, stop):
            mm(dst, w_h, m_h, start=start, stop=False, skip_group_check=True)
            mm(dst, w_h, m_l, start=False, stop=False, skip_group_check=True)
            return mm(dst, w_l, m_h, start=False, stop=stop, skip_group_check=True)

        def tile_out(bank0, j):
            return ps[:, bank0 + j // 2, (j % 2) * T:(j % 2 + 1) * T]

        def project_slice(s, bank0, rows, first, last, it=None, stride=0, before_bank=None):
            if it is None:
                pe.wait_ge(lo_ready, s + 1)
            else:
                pe.wait_ge(lo_ready, it * stride + (s + 1))
            for j in range(8):
                if j % 2 == 0 and before_bank:
                    before_bank(j // 2)
                w = slice(j * P, (j + 1) * P)
                ins = three(tile_out(bank0, j), w_hi[:, s % SPLIT, w], w_lo[:, s % SPLIT, w], h_hi[:, rows, :],
                            h_lo[:, rows, :], first and j % 2 == 0, last)
            ins.then_inc(slice_done, 1)

        def turn_ada(i, bank0, it=None):
            if it is None:
                pe.wait_ge(ada_used, 16 * (i + 1))
            else:
                pe.wait_ge(ada_used, it * 16 + 16 * (i + 1))
            for b in range(4):
                for f in range(4):
                    w = slice((4 * b + f) * P, (4 * b + f + 1) * P)
                    ins = nc.tensor.transpose(ps[:, bank0 + b, f * P:(f + 1) * P], ada_sum[:, w], ident[:, :])
                ins.then_inc(modT_ready, 1)

        def turn_half(it):
            pe.wait_ge(ada_used, it * 8 + (16 * HALVES + 8))
            for b in range(2):
                for f in range(4):
                    w = slice((4 * b + f) * P, (4 * b + f + 1) * P)
                    ins = nc.tensor.transpose(ps[:, b, f * P:(f + 1) * P], ada_sum[:, w], ident[:, :])
                ins.then_inc(modT_ready, 1)

        def sum_pair(n, bank, i):
            pe.wait_ge(sq_ready, 8 * n + i + 1)
            for k in range(2):
                ins = mm(ps[:, bank, 0:T], ones[:, :], sq[:, i % 2, k, :], start=(i == 0 and k == 0), stop=(i == 7 and k == 1))
            ins.then_inc(sq_used, 1)

        def sum_squares(n, bank):
            for i in range(8):
                sum_pair(n, bank, i)

        pe.wait_ge(small_in, 16 * 12)
        for i, n in enumerate((96, 96, N_MISC)):
            nc.tensor.transpose(ps[:, 0, i * P:i * P + n], vec_rows[0:n, i, :], ident[0:n, 0:n]).then_inc(vec_T, 1)

        def turn_rows(v):
            if v == 0:
                pe.wait_ge(x_in, 16)
                pe.wait_ge(vec_ready, 3)
            if v == 8:
                pe.wait_ge(ctx_rows_in, 16)
            if v >= 2:
                pe.wait_ge(rows_out, v - 1)
            src = x_rows if v < 8 else c_rows
            for k in range(2):
                for tt in range(2):
                    f = 2 * (v % 8) + k
                    ins = nc.tensor.transpose(ps[:, v % 2, k * T + tt * P:k * T + (tt + 1) * P], src[:, tt, f * P:(f + 1) * P],
                                              ident[:, :])
            ins.then_inc(rows_T, 1)

        pe.wait_ge(silu4_ready, 2)
        pe.wait_ge(ones_set, 1)
        for n in range(START):
            m, t = n // KT, n % KT
            if n == KT:
                pe.wait_ge(start_out, 1)
            for k in range(2):
                s = 2 * n + k
                pe.wait_ge(lo_ready, s + 1)
                for h in range(2):
                    bank, cols = 4 + 2 * k + h, slice(512 * h, 512 * (h + 1))
                    mm(ps[:, bank, :], silu4[:, t, :], w_hi[:, s % SPLIT, cols], start=(t == 0), stop=False)
                    ins = mm(ps[:, bank, :], silu4[:, t, :], w_lo[:, s % SPLIT, cols], start=False, stop=(t == KT - 1))
                ins.then_inc(slice_done, 1)
            if n < 16:
                turn_rows(n)
            if n >= 16:
                sum_pair((n - 16) // 8, 2 + (n - 16) // 8, n % 8)
        pe.wait_ge(start_out, 2)
        for f in range(2 * KT):
            ins = nc.tensor.transpose(ps[:, 0, 4 * f:4 * f + 4], start_rows[:, f * P:(f + 1) * P], ident[0:4, 0:4])
        ins.then_inc(start_T, 1)

        for s in range(16):
            if s % 2 == 0:
                pe.wait_ge(h_ready, s + 2)
            pe.wait_ge(lo_ready, 2 * P_KV + s + 1)
            for j in range(4):
                w = slice(j * P, (j + 1) * P)
                for st, (hh, hl) in enumerate(((h_hi, h_lo), (hc_hi, hc_lo))):
                    three(ps[:, j, st * T:(st + 1) * T], w_hi[:, s % SPLIT, w], w_lo[:, s % SPLIT, w], hh[:, s, :], hl[:, s, :],
                          s == 0 and st == 0, s == 15)
            for st in range(4):
                hh, hl = (h_hi, h_lo) if st < 2 else (hc_hi, hc_lo)
                tok = slice((st % 2) * P, (st % 2 + 1) * P)
                ins = three(ps[:, 4 + st, :], hh[:, s, tok], hl[:, s, tok], w_hi[:, s % SPLIT, 512:1024],
                            w_lo[:, s % SPLIT, 512:1024], s == 0, s == 15)
            ins.then_inc(slice_done, 1)
        pe.wait_ge(v_out, 4)
        turn_ada(0, 4)

        def head_ss(r, bank):
            pe.wait_ge(hsq_ready, r + 1)
            if r >= 1:
                pe.wait_ge(hrms_ready, r)
            if r >= 9:
                pe.wait_ge(head_ready, r)
            mm(ps[:, bank, :], ones[:, :], hsq[:, r % 2, :], start=True, stop=True).then_inc(hss_ready, 1)

        def head_swap(r, bank):
            pe.wait_ge(hnorm_ready, r + 1)
            if r >= 1:
                pe.wait_ge(head_ready, r)
            src = kT[:, r, :] if r < 4 else qT[:, 2 * (r - 4):2 * (r - 4) + 2, :].rearrange("p a t -> p (a t)")
            mm(ps[:, bank, :], swap[:, :], src, start=True, stop=True).then_inc(hswap_ready, 1)

        for b in range(2):
            for s in range(16):
                if s == 0 and b == 0:
                    pe.wait_ge(k_out, 4)
                if s == 0 and b == 1:
                    pe.wait_ge(head_ready, 4)
                if s % 4 == 1:
                    if s == 1 and b == 0:
                        pe.wait_ge(mod_part, 4)
                    if s == 1 and b == 1:
                        pe.wait_ge(q_out, 4)
                    head_ss(4 * b + s // 4, 5 if b == 0 else 1)
                if s % 4 == 0 and s:
                    head_swap(4 * b + s // 4 - 1, 6 if b == 0 else 2)
                project_slice(2 * P_Q + 16 * b + s, 4 * b, s, s == 0, s == 15)
            head_swap(4 * b + 3, 6 if b == 0 else 2)
        pe.wait_ge(head_ready, 8)
        turn_ada(1, 0)

        for n in range(36):
            if n < 32:
                h, qt = n // 2, n % 2
                if n == 0:
                    pe.wait_ge(q_out, 8)
                    pe.wait_ge(mod_part, 8)
                if n >= 3:
                    pe.wait_ge(exp_ready, n - 2)
                if n >= 16 and n % 4 == 0:
                    pe.wait_ge(head_ready, n // 4 + 5)
                mm(ps[:, n % 3, :], qT[:, h, qt * P:(qt + 1) * P], kT[:, h // 4, :], start=True, stop=True).then_inc(score_ready, 1)
            m = n - 2
            if 0 <= m < 32:
                pe.wait_ge(prob_ready, m + 1)
                if m >= 2:
                    pe.wait_ge(probT_out, m - 1)
                for st in range(4):
                    ins = nc.tensor.transpose(ps[:, 3 + m % 2, st * P:(st + 1) * P], prob[:, m % 3, st * P:(st + 1) * P], ident[:, :])
                ins.then_inc(probT_ready, 1)
            if n >= 4 and n % 2 == 0:
                h = (n - 4) // 2
                pe.wait_ge(probT_out, 2 * h + 2)
                if h >= 2:
                    pe.wait_ge(o_ready, h - 1)
                g = h // 4
                for st in range(4):
                    ins = mm(ps[:, 5 + h % 2, 0:T], vS[:, st, g * HD:(g + 1) * HD], probT[:, h % 2, st, :], start=(st == 0), stop=(st == 3))
                ins.then_inc(pv_ready, 1)
            if n % 3 == 1 and n <= 10:
                head_ss(8 + n // 3, 7)
            if n % 3 == 0 and 3 <= n <= 12:
                head_swap(8 + n // 3 - 1, 7)

        pe.wait_ge(exp_ready, 32)
        pe.wait_ge(probT_out, 32)
        turn_ada(2, 0)

        for l in range(2):
            n = 2 + 2 * l
            if l == 1:
                pe.wait_ge(mod_part, 4 * 7 + 4)
                sum_squares(3, 0)

                def stage1(g):
                    pe.wait_ge(h_ready, 24 + g + 1)
                    if g >= 2:
                        pe.wait_ge(z_ready, 2 * g - 2)
                    for nt in range(2):
                        tok = slice(nt * P, (nt + 1) * P)
                        for k in range(2):
                            ins = three(ps[:, 2 * (g % 2) + nt, :], h_hi[:, 2 * g + k, tok], h_lo[:, 2 * g + k, tok],
                                        dft_hi[:, k, 0:2 * T], dft_lo[:, k, 0:2 * T], k == 0, k == 1)
                        ins.then_inc(z_mm, 1)

                def stage2(g):
                    pe.wait_ge(z_ready, 2 * g + 2)
                    if g >= 2:
                        pe.wait_ge(y_ready, g - 1)
                    for ct in range(2):
                        for cs in range(2):
                            for nt in range(2):
                                c0 = cs * T + ct * P
                                r0 = cs * 2 * T
                                ins = three(ps[:, 4 + g % 2, ct * T:(ct + 1) * T], z_hi[:, g % 2, nt, c0:c0 + P],
                                            z_lo[:, g % 2, nt, c0:c0 + P], dft_hi[:, nt, r0:r0 + T], dft_lo[:, nt, r0:r0 + T],
                                            ct == 0 and cs == 0 and nt == 0, cs == 1 and nt == 1)
                    ins.then_inc(y_mm, 1)

                pe.wait_ge(dft_ready, 1)
                pe.wait_ge(rms_ready, 4)
                pe.wait_ge(mod_ready, mods_ready(7))
                pe.wait_ge(x_added, 32)
                stage1(0)
                for g in range(8):
                    if g + 1 < 8:
                        stage1(g + 1)
                    stage2(g)
            for b in range(2):
                for s in range(16):
                    if l == 0:
                        if b == 0:
                            pe.wait_ge(o_ready, s + 1)
                    else:
                        if s == 0 and b == 0:
                            pe.wait_ge(z_ready, 16)
                        if b == 0:
                            pe.wait_ge(y_ready, s // 2 + 1)
                    hook = None
                    if l == 0 and b == 0 and s == 0:
                        def hook(bank):
                            pe.wait_ge(mod_part, 4 * 2 + bank + 1)
                    project_slice(2 * P_WO[l] + 16 * b + s, 4 * b, s, s == 0, s == 15, before_bank=hook)
            pe.wait_ge(x_added, 8 + 32 * l)
            s0 = 3 if l == 0 else 8
            turn_ada(s0, 0)
            pe.wait_ge(x_added, 10 + 32 * l)
            sum_squares(n, 4)
            pe.wait_ge(x_added, 16 + 32 * l)
            pe.wait_ge(mod_part, 4 * s0 + 4)
            pe.wait_ge(rms_ready, n + 1)
            with pe.Fori(0, 4) as it:
                for b in range(2):
                    for s in range(16):
                        if s % 2 == 0:
                            pe.wait_ge(h_ready, 8 * n + s // 2 + 1)
                        hook = None
                        if s == 0 and b == 0 and l == 0:
                            def hook(bank):
                                if bank < 2:
                                    pe.wait_ge(mod_part, it * 2 + (4 * HALVES - 1 + bank))
                        project_slice(2 * P_UP[l] + 16 * b + s, 4 * b, s, s == 0, s == 15, it, 32, hook)
                    pe.wait_ge(u_ready, it * 2 + (8 * l + b + 1))
                if l == 0:
                    turn_half(it)
            for sw in range(2):
                first = 2 * P_DOWN[l] + 64 * sw

                def group(g, i0, head, tail):
                    for i in range(4):
                        piece = i0 + i
                        if tail and i == 3 and sw == 1 and l == 0:
                            pe.wait_ge(x_added, 24)
                            turn_ada(7, 0)
                        if g is None:
                            pe.wait_ge(ulo_ready, 64 * l + 32 * sw + piece + 1)
                        else:
                            pe.wait_ge(ulo_ready, g * 4 + (64 * l + 32 * sw + piece + 1))
                        for k in range(2):
                            hook = None
                            if head and i == 0 and k == 0 and (l, sw) != (1, 0):
                                def hook(bank):
                                    if sw == 1:
                                        pe.wait_ge(mod_part, 4 * (6 if l == 0 else 9) + bank + 1)
                                    elif bank < 2:
                                        pe.wait_ge(mod_part, 4 * 6 - 1 + bank)
                            project_slice(first + 2 * piece + k, 4 * sw, 2 * i + k, head and i == 0 and k == 0,
                                          tail and i == 3 and k == 1, g, 8, hook)

                pe.wait_ge(u_ready, 8 * l + 8 + sw)
                group(None, 0, True, False)
                with pe.Fori(1, 7) as g:
                    group(g, 0, False, False)
                group(None, 28, False, True)
                if sw == 0:
                    pe.wait_ge(u_ready, 8 * l + 9)
                    turn_ada(6 if l == 0 else 9, 4)
            pe.wait_ge(x_added, 24 + 32 * l)
        sum_squares(5, 0)
        pe.wait_ge(x_added, 64)
        for tt in range(2):
            for i in range(4):
                v = 4 * tt + i
                if tt == 0:
                    pe.wait_ge(fin_ready, 4 * i + 4)
                if v >= 4:
                    pe.wait_ge(fin_out, v - 3)
                for k in range(4):
                    ins = nc.tensor.transpose(ps[:, 1 + v % 4, k * P:(k + 1) * P], yT[:, 4 * i + k, tt * P:(tt + 1) * P], ident[:, :])
                ins.then_inc(fin_T, 1)

    stack.close()


def constants():
    ident = np.eye(P, dtype=np.float32)
    swap = np.zeros((P, P), np.float32)
    for i in range(0, P, 2):
        swap[i + 1, i] = -1.0
        swap[i, i + 1] = 1.0
    n_freq = HD // 4
    inv = (np.float32(10000.0) ** (-np.arange(n_freq, dtype=np.float32) / np.float32(n_freq))).astype(np.float32)
    tok = np.arange(T)
    row, col = (tok // GRID_W).astype(np.float32), (tok % GRID_W).astype(np.float32)
    ang = np.concatenate([row[:, None] * inv, col[:, None] * inv], axis=1)
    ang = np.repeat(ang.T, 2, axis=0).astype(np.float64)
    rope = np.stack([np.cos(ang), np.sin(ang)]).astype(np.float32)
    k = np.outer(np.arange(T), np.arange(T)) % T
    th = 2.0 * np.pi * k / T
    dft = np.concatenate([np.cos(th), np.sin(th), -np.sin(th)], axis=1).astype(np.float32)
    return ident, swap, rope, dft


_INS = ["x", "c", "ctx", "c_ctx", "ada_w", "ada_b", "norm_mix_g", "norm_mlp_g", "attn_w_qkv", "attn_q_norm_g",
        "attn_k_norm_g", "attn_w_o", "fourier_w_o", "mlp_w1", "mlp_w2", "final_norm_g"]


def kernel(**inputs):
    import numpy as _np
    import concourse.bacc as _bacc
    from concourse import mybir as _mybir
    from concourse.bass_utils import run_bass_kernel_spmd as _run

    nc = _bacc.Bacc("TRN2", target_bir_lowering=False, num_devices=1)
    arrays, args = {}, []
    for name in _INS:
        a = _np.ascontiguousarray(inputs[name])
        arrays[f"in_{name}"] = a
        args.append(nc.dram_tensor(f"in_{name}", a.shape, _mybir.dt.from_np(a.dtype), kind="ExternalInput").ap())
    for name, a in zip(("ident", "swap", "rope", "dft"), constants()):
        arrays[f"const_{name}"] = a
        args.append(nc.dram_tensor(f"const_{name}", a.shape, _mybir.dt.from_np(a.dtype), kind="ExternalInput").ap())
    args.append(nc.dram_tensor("out_0", (1, T, D), _mybir.dt.float32, kind="ExternalOutput").ap())
    layer_block(nc, *args)
    r = _run(nc, [arrays], core_ids=[0])
    return r.results[0]["out_0"]
```
